# Optimizing a Trainium2 kernel written in Bass

```python
import jax, jax.numpy as jnp
from jax import lax
import numpy as np

D_MODEL = 2048
BATCH = 1
SEQ = 256
DEPTH = 2

N_MIXERS = 3
N_CONV_LAYERS = len(range(0, DEPTH, N_MIXERS))
N_GLA_LAYERS = len(range(1, DEPTH, N_MIXERS))
N_RET_LAYERS = len(range(2, DEPTH, N_MIXERS))
NORM_EPS = 1e-6
D_FF = -(-8 * D_MODEL // (3 * 256)) * 256
CONV_WIDTH = 3
GLA_HEADS = 4
GLA_KEY_DIM = D_MODEL // 2
GLA_DK = GLA_KEY_DIM // GLA_HEADS
GLA_DV = D_MODEL // GLA_HEADS
GLA_GATE_RANK = 16
GLA_GATE_TAU = 16.0
GLA_CHUNK = 64
GLA_IN_WIDTH = 2 * GLA_KEY_DIM + 2 * D_MODEL + GLA_GATE_RANK
RET_HEADS = 8
RET_DK = D_MODEL // RET_HEADS
RET_VALUE_FACTOR = 2
RET_V_WIDTH = RET_VALUE_FACTOR * D_MODEL
RET_DV = RET_V_WIDTH // RET_HEADS
RET_CHUNK = 128
RET_IN_WIDTH = 2 * D_MODEL + 2 * RET_V_WIDTH
ROPE_BASE = 10000.0

kernel_name = "hybrid_conv_gla_retention_trunk"

def _rmsnorm(x, g):
    xf = x.astype(jnp.float32)
    y = xf * lax.rsqrt(jnp.mean(xf * xf, axis=-1, keepdims=True) + NORM_EPS)
    return (y * g.astype(jnp.float32)).astype(x.dtype)

def _head_rmsnorm(o):
    return o * lax.rsqrt(jnp.mean(o * o, axis=-1, keepdims=True) + NORM_EPS)

def _to_chunks(t, chunk):
    b, s, h, d = t.shape
    return t.reshape(b, s // chunk, chunk, h, d).transpose(0, 3, 1, 2, 4)

def _from_chunks(o):
    b, h, n, c, d = o.shape
    return o.transpose(0, 2, 3, 1, 4).reshape(b, n * c, h * d)

def _inter_chunk(q_in, k_in, v, decay):
    b, h, _, _, dk = q_in.shape
    dv = v.shape[-1]

    def step(state, xs):
        qc, kc, vc, dc = xs
        out = jnp.einsum('bhcd,bhde->bhce', qc, state)
        state = state * dc[..., None] + jnp.einsum('bhcd,bhce->bhde', kc, vc)
        return state, out

    state0 = jnp.zeros((b, h, dk, dv), jnp.float32)
    xs = tuple(jnp.moveaxis(a, 2, 0) for a in (q_in, k_in, v, decay))
    _, out = lax.scan(step, state0, xs)
    return jnp.moveaxis(out, 0, 2)

def _short_conv_mixer(h, w_in, w_conv, w_out):
    proj = h @ w_in
    gate_b, gate_c, u = jnp.split(proj, 3, axis=-1)
    u = gate_c * u
    conv = lax.conv_general_dilated(
        u, w_conv[:, None, :].astype(u.dtype), window_strides=(1,),
        padding=[(CONV_WIDTH - 1, 0)], dimension_numbers=('NWC', 'WIO', 'NWC'),
        feature_group_count=D_MODEL)
    return (gate_b * conv) @ w_out

def _gla_mixer(h, w_in, w_gate2, b_gate, g_norm, w_out):
    b, s, _ = h.shape
    proj = h @ w_in
    q, k, v, r, z = jnp.split(
        proj, [GLA_KEY_DIM, 2 * GLA_KEY_DIM, 2 * GLA_KEY_DIM + D_MODEL,
               2 * GLA_KEY_DIM + 2 * D_MODEL], axis=-1)
    log_a = jax.nn.log_sigmoid((z @ w_gate2 + b_gate).astype(jnp.float32)) / GLA_GATE_TAU
    f32 = jnp.float32
    q = _to_chunks(q.astype(f32).reshape(b, s, GLA_HEADS, GLA_DK), GLA_CHUNK) * GLA_DK ** -0.5
    k = _to_chunks(k.astype(f32).reshape(b, s, GLA_HEADS, GLA_DK), GLA_CHUNK)
    v = _to_chunks(v.astype(f32).reshape(b, s, GLA_HEADS, GLA_DV), GLA_CHUNK)
    g = _to_chunks(log_a.reshape(b, s, GLA_HEADS, GLA_DK), GLA_CHUNK)
    cum = jnp.cumsum(g, axis=-2)
    cum_last = cum[..., -1:, :]
    q_t = q * jnp.exp(cum)
    k_t = k * jnp.exp(-cum)
    k_end = k * jnp.exp(cum_last - cum)
    causal = jnp.tril(jnp.ones((GLA_CHUNK, GLA_CHUNK), bool))
    att = jnp.where(causal, jnp.einsum('bhncd,bhnsd->bhncs', q_t, k_t), 0.0)
    o = jnp.einsum('bhncs,bhnse->bhnce', att, v)
    o = o + _inter_chunk(q_t, k_end, v, jnp.exp(cum_last[..., 0, :]))
    o = _head_rmsnorm(o) * g_norm.astype(f32)
    o = _from_chunks(o).astype(h.dtype)
    return (jax.nn.silu(r) * o) @ w_out

def _rotary(t, cos, sin):
    half = t.shape[-1] // 2
    rot = jnp.concatenate([-t[..., half:], t[..., :half]], axis=-1)
    return t * cos[:, None, :] + rot * sin[:, None, :]

def _retention_mixer(h, w_in, w_out):
    b, s, _ = h.shape
    f32 = jnp.float32
    proj = h @ w_in
    q, k, v, g = jnp.split(proj, [D_MODEL, 2 * D_MODEL, 2 * D_MODEL + RET_V_WIDTH], axis=-1)
    pos = jnp.arange(s, dtype=f32)
    inv_freq = 1.0 / (ROPE_BASE ** jnp.linspace(0.0, 1.0, RET_DK // 2, dtype=f32))
    ang = pos[:, None] * inv_freq[None, :]
    cos = jnp.cos(jnp.concatenate([ang, ang], axis=-1))
    sin = jnp.sin(jnp.concatenate([ang, ang], axis=-1))
    q = _to_chunks(_rotary(q.astype(f32).reshape(b, s, RET_HEADS, RET_DK), cos, sin), RET_CHUNK)
    k = _to_chunks(_rotary(k.astype(f32).reshape(b, s, RET_HEADS, RET_DK), cos, sin), RET_CHUNK) * RET_DK ** -0.5
    v = _to_chunks(v.astype(f32).reshape(b, s, RET_HEADS, RET_DV), RET_CHUNK)
    log_gamma = jnp.log(1.0 - 2.0 ** (-5.0 - jnp.arange(RET_HEADS, dtype=f32)))
    idx = jnp.arange(RET_CHUNK, dtype=f32)
    rel = idx[:, None] - idx[None, :]
    dmat = jnp.where(rel >= 0, jnp.exp(jnp.maximum(rel, 0.0)[None] * log_gamma[:, None, None]), 0.0)
    scores = jnp.einsum('bhncd,bhnsd->bhncs', q, k) * dmat[None, :, None]
    o = jnp.einsum('bhncs,bhnse->bhnce', scores, v)
    lg = log_gamma[None, :, None, None, None]
    q_in = q * jnp.exp(lg * (idx + 1.0)[:, None])
    k_in = k * jnp.exp(lg * (RET_CHUNK - 1.0 - idx)[:, None])
    n = q.shape[2]
    decay = jnp.broadcast_to(jnp.exp(log_gamma * RET_CHUNK)[None, :, None, None], (b, RET_HEADS, n, 1))
    o = o + _inter_chunk(q_in, k_in, v, decay)
    o = _from_chunks(_head_rmsnorm(o)).astype(h.dtype)
    return (jax.nn.silu(g) * o) @ w_out

def _swiglu(h, w_in, w_out):
    gate, up = jnp.split(h @ w_in, 2, axis=-1)
    return (jax.nn.silu(gate) * up) @ w_out

def setup_inputs(seed: int = 0) -> dict:
    key = jax.random.key(seed)
    ks = jax.random.split(key, 17)
    f32 = jnp.float32
    nrm = lambda k, shape, scale: jax.random.normal(k, shape, f32) * scale
    D = D_MODEL
    return {
        "x": nrm(ks[0], (BATCH, SEQ, D), 1.0),
        "norm_mix": 1.0 + nrm(ks[1], (DEPTH, D), 0.02),
        "norm_ffn": 1.0 + nrm(ks[2], (DEPTH, D), 0.02),
        "norm_final": 1.0 + nrm(ks[3], (D,), 0.02),
        "conv_w_in": nrm(ks[4], (N_CONV_LAYERS, D, 3 * D), D ** -0.5),
        "conv_w": nrm(ks[5], (N_CONV_LAYERS, CONV_WIDTH, D), CONV_WIDTH ** -0.5),
        "conv_w_out": nrm(ks[6], (N_CONV_LAYERS, D, D), D ** -0.5),
        "gla_w_in": nrm(ks[7], (N_GLA_LAYERS, D, GLA_IN_WIDTH), D ** -0.5),
        "gla_w_gate2": nrm(ks[8], (N_GLA_LAYERS, GLA_GATE_RANK, GLA_KEY_DIM), GLA_GATE_RANK ** -0.5),
        "gla_b_gate": nrm(ks[9], (N_GLA_LAYERS, GLA_KEY_DIM), 0.1),
        "gla_norm": 1.0 + nrm(ks[10], (N_GLA_LAYERS, GLA_DV), 0.02),
        "gla_w_out": nrm(ks[11], (N_GLA_LAYERS, D, D), D ** -0.5),
        "ret_w_in": nrm(ks[12], (N_RET_LAYERS, D, RET_IN_WIDTH), D ** -0.5),
        "ret_w_out": nrm(ks[13], (N_RET_LAYERS, RET_V_WIDTH, D), RET_V_WIDTH ** -0.5),
        "ffn_w_in": nrm(ks[14], (DEPTH, D, 2 * D_FF), D ** -0.5),
        "ffn_w_out": nrm(ks[15], (DEPTH, D_FF, D), D_FF ** -0.5),
    }

def reference(x, norm_mix, norm_ffn, norm_final, conv_w_in, conv_w, conv_w_out,
              gla_w_in, gla_w_gate2, gla_b_gate, gla_norm, gla_w_out,
              ret_w_in, ret_w_out, ffn_w_in, ffn_w_out):
    for i in range(DEPTH):
        h = _rmsnorm(x, norm_mix[i])
        kind, j = i % N_MIXERS, i // N_MIXERS
        if kind == 0:
            mix = _short_conv_mixer(h, conv_w_in[j], conv_w[j], conv_w_out[j])
        elif kind == 1:
            mix = _gla_mixer(h, gla_w_in[j], gla_w_gate2[j], gla_b_gate[j], gla_norm[j], gla_w_out[j])
        else:
            mix = _retention_mixer(h, ret_w_in[j], ret_w_out[j])
        x = x + mix
        x = x + _swiglu(_rmsnorm(x, norm_ffn[i]), ffn_w_in[i], ffn_w_out[i])
    return _rmsnorm(x, norm_final)


_drawn_inputs = setup_inputs


def setup_inputs(seed=0):
    import zlib

    import numpy as np

    out = dict(_drawn_inputs(seed))
    spreads = {}
    factors = {'norm_ffn': 3.257, 'norm_final': 2.943, 'gla_b_gate': 3.414, 'gla_norm': 7.026}
    for name, (base, spread) in spreads.items():
        noise = np.random.default_rng([zlib.crc32(name.encode()), seed]).standard_normal(out[name].shape)
        drawn = base * np.exp(spread * noise) if base else spread * noise
        out[name] = __import__('jax').numpy.asarray(drawn.astype(out[name].dtype))
    for name, factor in factors.items():
        out[name] = (out[name] * factor).astype(out[name].dtype)
    return out
```

```python
import concourse.bass as bass
from concourse import mybir
from contextlib import ExitStack


P = 128
T = 256
D = 2048
DT = D // P
GW = 512
GT = GW // P
F = 5632
PAIRS = F // GW
PIECES = (4, 4, 3)
HEADS, DK, DV, CHUNK, RANK = 4, 256, 512, 64, 16
KEY = HEADS * DK
NCHUNK = T // CHUNK
GLA_COLS = 2 * KEY + 2 * D + RANK
EPS = 1e-6
TAU = 16.0
SLOTS = 4
SUB_K = 2

V_MIX, V_FFN, V_FINAL, V_CONV, V_BIAS, V_HEAD = 0, 2 * DT, 4 * DT, 5 * DT, 8 * DT, 8 * DT + KEY // P

ADDS = {
    "ingest": dict(half_free=1, xs_hi=1, squares=1, xs_ready=1, sumsq=1),
    "partial": dict(half_free=1, x_added=1),
    "finish": dict(half_free=1, x_added=1, xs_hi=1, squares=1, xs_ready=1, sumsq=1),
    "conv_c": dict(half_free=1, scaled=1),
    "conv_u": dict(half_free=1, scaled=1, taps=3),
    "conv_b": dict(half_free=1, scaled=1, product=1, mid_hi=1, mid_ready=1),
    "gate": dict(half_free=1, scaled=1, silu=1),
    "up": dict(half_free=1, scaled=1, product=1, mid_hi=1, mid_ready=1),
    "key": dict(half_free=1, scaled=1),
    "query": dict(half_free=1, scaled=1),
    "zed": dict(half_free=1, scaled=1),
    "logits": dict(half_free=1),
    "value": dict(half_free=1),
    "scores": dict(half_free=1),
    "head": dict(half_free=1, product=1, mid_hi=1, mid_ready=1),
    "store": dict(half_free=1),
}
NO_WEIGHTS = ("ingest", "logits", "scores", "head", "store")


def schedule():
    groups = [("ingest", 0, "ingest")] * 4
    groups += [("conv_c", 8, "conv_in"), ("conv_u", 8, "conv_in"), ("conv_b", 8, "conv_in")] * 4
    groups += [("finish", 8, "conv_out")] * 4

    def ffn(layer):
        out = []
        for n, pairs in enumerate(PIECES):
            out += [("gate", 8, f"ffn{layer}_in{n}"), ("up", 8, f"ffn{layer}_in{n}")] * pairs
            kind = "finish" if n == len(PIECES) - 1 else "partial"
            out += [(kind, 2 * pairs, f"ffn{layer}_out{n}")] * 4
        return out

    groups += ffn(0)
    for kind in ("key", "zed", "key", "logits", "query", "query", "value", "value", "value", "value",
                 "gate", "scores", "gate", "head", "gate", "head", "gate", "head", "head"):
        groups.append((kind, 0 if kind in NO_WEIGHTS else 2 if kind == "zed" else 8, "gla_in"))
    groups += [("finish", 8, "gla_out")] * 4
    groups += ffn(1)
    groups += [("store", 0, "store")] * 4
    return groups


GROUPS = schedule()


def first_of(phase):
    return [p for _, _, p in GROUPS].index(phase)


def count_of(phase):
    return sum(p == phase for _, _, p in GROUPS)


def sub_before(g):
    return sum(s for _, s, _ in GROUPS[:g])


def before(name, g):
    return sum(ADDS[k].get(name, 0) for k, _, _ in GROUPS[:g])


class At:

    def __init__(self, g, turn=0, cycle=0):
        self.g, self.turn, self.cycle = g, turn, cycle
        self.half = g % 2

    def value(self, name, more):
        step = before(name, self.g + self.cycle) - before(name, self.g)
        return before(name, self.g) + more + (self.turn * step if self.cycle else 0)

    def subs_done(self):
        step = sub_before(self.g + self.cycle) - sub_before(self.g)
        return sub_before(self.g + 1) + (self.turn * step if self.cycle else 0)

    def groups_done(self, more):
        return self.g + more + (self.turn * self.cycle if self.cycle else 0)


def trunk(nc, x, norm_mix, norm_ffn, norm_final, conv_w_in, conv_w, conv_w_out, gla_w_in, gla_w_gate2,
          gla_b_gate, gla_norm, gla_w_out, ffn_w_in, ffn_w_out, out):
    f32, f32r = mybir.dt.float32, mybir.dt.float32r
    ACT, ALU, AX = mybir.ActivationFunctionType, mybir.AluOpType, mybir.AxisListType
    ctx = ExitStack()
    with ctx:
        def sb(name, shape, dt=f32, where=None):
            return (where or ctx).enter_context(nc.sbuf_tensor(name, shape, dt))

        def sem(name):
            return ctx.enter_context(nc.semaphore(name))

        xT = sb("xT", [P, DT, T])
        xs = sb("xs", [P, DT, 2 * T], f32r)
        raw = sb("raw", [P, SLOTS, 4, GW])
        w_hi = sb("w_hi", [P, SLOTS, SUB_K, GW], f32r)
        w_lo = sb("w_lo", [P, SLOTS, SUB_K, GW], f32r)
        summed = sb("summed", [P, GT, T])
        work = sb("work", [P, GT, T])
        sum_x = sb("sum_x", [P, T])
        sum_group = sb("sum_group", [P, T])
        rstd = sb("rstd", [P, T + 2])
        rstd_sq = sb("rstd_sq", [P, T])
        vec = sb("vec", [P, V_HEAD + DV // P])
        ident = sb("ident", [P, P])
        mean_x = sb("mean_x", [P, P])
        mean_head = sb("mean_head", [P, P])

        with ExitStack() as use:
            q_far = sb("q_far", [P, KEY // P, 3, CHUNK], where=use)
            w_gate2 = sb("w_gate2", [P, KEY], where=use)
            zT = sb("zT", [P, T], where=use)
            decay = sb("decay", [P, KEY // P, NCHUNK], where=use)
            reset = sb("reset", [P, T], where=use)
            pad_words = (DT * T - KEY // P * 3 * CHUNK - KEY - T - KEY // P * NCHUNK - T)
            sb("unused", [P, pad_words], where=use)
            r_act = sb("r_act", [P, DT, T], where=use)
        mid = sb("mid", [P, DT, 2 * T], f32r)

        with ExitStack() as use:
            x_tok = sb("x_tok", [P, 2, D], where=use)
            rows_a = sb("rows_a", [P, P], where=use)
            rows_b = sb("rows_b", [KEY // P + DV // P, P], where=use)
        with ExitStack() as use:
            conv_gate = sb("conv_gate", [P, GT, T], where=use)
            conv_in = sb("conv_in", [P, GT, T + 2], where=use)
            conv_y = sb("conv_y", [P, GT, T], where=use)
        with ExitStack() as use:
            y_norm = sb("y_norm", [P, DT, T], where=use)
            y_tok = sb("y_tok", [P, 2, D], where=use)
        cum = sb("cum", [P, KEY // P, T])
        q_t = sb("q_t", [P, KEY // P, T])
        k_t = sb("k_t", [P, KEY // P, T])
        k_end = sb("k_end", [P, KEY // P, T])
        v_tok = sb("v_tok", [P, 2, D])
        att = cum[:, :, :].rearrange("p a t -> p (a t)")[:, 0:HEADS * 3 * P].rearrange("p (h c) -> p h c", h=HEADS)
        head_out = k_t[:, :, :].rearrange("p (a e) t -> p a e t", a=2)

        ps = ctx.enter_context(nc.psum_tensor("ps", [P, 8, GW], f32))

        raw_loaded = [sem(f"raw_loaded{i}") for i in range(SLOTS)]
        hi_ready = sem("hi_ready")
        lo_ready = sem("lo_ready")
        sub_done = sem("sub_done")
        x_loaded = [sem(f"x_loaded{j}") for j in range(4)]
        vectors_loaded = sem("vectors_loaded")
        gate2_loaded = sem("gate2_loaded")
        consts_ready = sem("consts_ready")
        vectors_turned = sem("vectors_turned")
        vectors_ready = sem("vectors_ready")
        turned = sem("turned")
        s = {n: sem(n) for n in ("half_free", "x_added", "xs_hi", "squares", "xs_ready", "sumsq", "scaled",
                                 "taps", "product", "mid_hi", "mid_ready", "silu")}
        group_summed = sem("group_summed")
        mean_done = sem("mean_done")
        ms_ready = sem("ms_ready")
        root_ready = sem("root_ready")
        rstd_ready = sem("rstd_ready")
        rstd_sq_ready = sem("rstd_sq_ready")
        conv_edge = sem("conv_edge")
        zed_done = sem("zed_done")
        gate2_padded = sem("gate2_padded")
        reset_ready = sem("reset_ready")
        logits_done = sem("logits_done")
        log1p_steps = sem("log1p_steps")
        log_decay_ready = sem("log_decay_ready")
        cum_ready = sem("cum_ready")
        exp_cum = sem("exp_cum")
        tail_ready = sem("tail_ready")
        tail_exp = sem("tail_exp")
        decay_ready = sem("decay_ready")
        keys_ready = sem("keys_ready")
        q_ready = sem("q_ready")
        q_far_steps = sem("q_far_steps")
        scores_done = sem("scores_done")
        att_masked = sem("att_masked")
        head_done = sem("head_done")
        head_copied = sem("head_copied")
        head_squares = sem("head_squares")
        head_sumsq = sem("head_sumsq")
        head_mean = sem("head_mean")
        head_root = sem("head_root")
        head_rstd = sem("head_rstd")
        head_scaled = sem("head_scaled")
        y_ready = sem("y_ready")
        y_copied = [sem("y_copied0"), sem("y_copied1")]
        stored = sem("stored")

        def bank(half, b):
            return ps[:, 4 * half + b, :]

        def two_parts(half):
            return ps[:, 4 * half:4 * half + 4, :].rearrange("p b (h t) -> p b t h", h=2)

        def packed(half, tiles):
            return ps[:, 4 * half:4 * half + tiles // 2, :].rearrange("p b (a t) -> p (b a) t", a=2)

        GAIN = [V_MIX, V_FFN, V_MIX + DT, V_FFN + DT, V_FINAL]
        FINISH_GROUPS = [g for g, (k, _, _) in enumerate(GROUPS) if k in ("ingest", "finish")]

        block = ctx.enter_context(nc.Block())

        @block.sync
        def _(sp):
            def chunk(c, src, turn=0, step=0, view=None):
                slot = c % SLOTS
                if c >= SLOTS or step:
                    sp.wait_ge(lo_ready, 2 * (c - SLOTS) + 2 + (turn * (2 * step) if step else 0))
                dst = raw[:, slot] if view is None else raw[:, slot].rearrange("p a n -> p (a n)")\
                    .rearrange("p (k n) -> p k n", n=view)
                sp.dma_start(dst, src).then_inc(raw_loaded[slot], 16)

            def matrix(w):
                return w.rearrange("(k p) n -> p k n", p=P)

            def group(c, w, k0, kn, col, turn=0, step=0):
                for n in range(kn // 4):
                    chunk(c + n, w[:, k0 + 4 * n:k0 + 4 * n + 4, bass.ds(col, GW)], turn, step)
                return c + kn // 4

            c = 0
            w = matrix(conv_w_in)
            for part in (1, 2, 0):
                c = group(c, w, 0, DT, part * D)
            with sp.Fori(0, D // GW - 1) as i:
                for n, part in enumerate((1, 2, 0)):
                    group(c + 4 * n, w, 0, DT, i * GW + (part * D + GW), i, 12)
            c += 12 * (D // GW - 1)
            with sp.Fori(0, D // GW) as i:
                group(c, matrix(conv_w_out), 0, DT, i * GW, i, 4)
            c += 4 * (D // GW)

            def ffn(c, layer):
                w_in, w_out = matrix(ffn_w_in[layer]), matrix(ffn_w_out[layer])
                k0 = 0
                for pairs in PIECES:
                    with sp.Fori(0, pairs) as i:
                        group(c, w_in, 0, DT, i * GW + k0 * P, i, 8)
                        group(c + 4, w_in, 0, DT, i * GW + (F + k0 * P), i, 8)
                    c += 8 * pairs
                    if pairs == SLOTS:
                        with sp.Fori(0, D // GW) as i:
                            group(c, w_out, k0, 4 * pairs, i * GW, i, pairs)
                        c += pairs * (D // GW)
                    else:
                        for n in range(D // GW):
                            c = group(c, w_out, k0, 4 * pairs, n * GW)
                    k0 += 4 * pairs
                return c

            c = ffn(c, 0)
            w = matrix(gla_w_in)
            c = group(c, w, 0, DT, KEY)
            chunk(c, w[:, :, GLA_COLS - P:GLA_COLS], view=P)
            c = group(c + 1, w, 0, DT, KEY + GW)
            for col in (0, GW):
                c = group(c, w, 0, DT, col)
            with sp.Fori(0, 2 * D // GW) as i:
                group(c, w, 0, DT, i * GW + 2 * KEY, i, 4)
            c += 4 * (2 * D // GW)
            with sp.Fori(0, D // GW) as i:
                group(c, matrix(gla_w_out), 0, DT, i * GW, i, 4)
            c += 4 * (D // GW)
            ffn(c, 1)
            for j in range(4):
                sp.wait_ge(y_copied[0], j + 1)
                sp.wait_ge(y_copied[1], j + 1)
                sp.dma_start(out.rearrange("(m p) n -> p m n", p=P)[:, :, j * GW:(j + 1) * GW],
                             y_tok[:, :, j * GW:(j + 1) * GW]).then_inc(stored, 16)
            sp.wait_ge(stored, 4 * 16)

        @block.gpsimd
        def _(pool):
            pool.memset(ident[:, :], 0.0).then_inc(consts_ready, 1)
            pool.memset(mean_x[:, :], 1.0 / D).then_inc(consts_ready, 1)
            pool.memset(mean_head[:, :], 1.0 / DV).then_inc(consts_ready, 1)
            pool.wait_ge(consts_ready, 3)
            pool.affine_select(out=ident[:, :], in_=ident[:, :], compare_op=ALU.not_equal, fill=1.0, base=0,
                               pattern=[[-1, P]], channel_multiplier=1).then_inc(consts_ready, 1)
            pool.wait_ge(s["half_free"], first_of("gla_in") + 12)
            pool.affine_select(out=att[:, :, 0:T], in_=att[:, :, 0:T], compare_op=ALU.is_ge, fill=0.0, base=0,
                               pattern=[[0, HEADS], [1, T]], channel_multiplier=-1).then_inc(att_masked, 1)
            pool.affine_select(out=att[:, :, T:3 * P], in_=att[:, :, T:3 * P], compare_op=ALU.is_ge, fill=0.0,
                               base=0, pattern=[[0, HEADS], [1, P]], channel_multiplier=-1).then_inc(att_masked, 1)

        def run(eng, split, pending, g0, n, evacs, looped, after_first=None):
            cycle = len(evacs)
            turns = n // cycle

            def one(g, readout, turn=0, stride=0):
                subs = GROUPS[g][1]
                split(g, 0, min(4, subs), turn, stride)
                readout()
                split(g, min(4, subs), subs, turn, stride)

            one(g0, pending)
            if after_first:
                after_first()
            if looped and turns > 2:
                with eng.Fori(0, turns - 1) as i:
                    for q in range(1, cycle + 1):
                        one(g0 + q, lambda: evacs[q - 1](At(g0 + q - 1, i, cycle)), i, cycle)
            else:
                for q in range(1, (turns - 1) * cycle + 1):
                    one(g0 + q, lambda: evacs[(q - 1) % cycle](At(g0 + q - 1)))
            last = g0 + (turns - 1) * cycle
            for q in range(1, cycle):
                one(last + q, lambda: evacs[q - 1](At(last + q - 1)))
            return lambda: evacs[cycle - 1](At(last + cycle - 1))

        def sub_number(g, n, turn, stride):
            return sub_before(g) + n, turn * (sub_before(g + stride) - sub_before(g)) if stride else 0

        def raw_view(i):
            return raw[:, i // 2 % SLOTS, SUB_K * (i % 2):SUB_K * (i % 2) + SUB_K, :]

        def mid_tiles(at, phase_first, per):
            t0 = (at.g - phase_first) // per * GT
            if at.cycle:
                return bass.ds(at.turn * (at.cycle // per * GT) + t0, GT)
            return slice(t0, t0 + GT)

        def whole_program(eng, split, e):
            nothing = lambda: None
            pend = nothing
            for j in range(4):
                pend()
                pend = (lambda j: lambda: e.ingest(At(j), j))(j)

            def finish(norm):
                return lambda at: e.finish(at, norm)

            g = first_of("conv_in")
            pend = run(eng, split, pend, g, 12, [e.conv_c, e.conv_u, e.conv_b] * 2, False, lambda: e.norm(0))
            pend = run(eng, split, pend, first_of("conv_out"), 4, [finish(1)] * 2, False)

            def ffn(layer, pend):
                for n, pairs in enumerate(PIECES):
                    g = first_of(f"ffn{layer}_in{n}")
                    up = (lambda g: lambda at: e.up(at, g))(g)
                    pend = run(eng, split, pend, g, 2 * pairs, [e.gate, up], True,
                               (lambda: e.norm(2 * layer + 1)) if n == 0 else None)
                    last = n == len(PIECES) - 1
                    pend = run(eng, split, pend, first_of(f"ffn{layer}_out{n}"), 4,
                               [finish(2 * layer + 2) if last else e.partial] * 2, False)
                return pend

            pend = ffn(0, pend)
            g = first_of("gla_in")
            K0, Z, K1, Y, Q0, Q1, V0, R0, S = g, g + 1, g + 2, g + 3, g + 4, g + 5, g + 6, g + 10, g + 11
            R1, H0, R2, H1, R3, H2, H3 = range(g + 12, g + 19)

            def weights_of(group, *readouts):
                subs = GROUPS[group][1]
                split(group, 0, min(4, subs), 0, 0)
                for r in readouts:
                    r()
                split(group, min(4, subs), subs, 0, 0)

            weights_of(K0, pend)
            e.norm(2)
            weights_of(Z)
            weights_of(K1, lambda: e.key(At(K0), 0), lambda: e.zed(At(Z)))
            weights_of(Q0, lambda: e.key(At(K1), 1), lambda: e.logits(At(Y)))
            weights_of(Q1, lambda: e.query(At(Q0), 0), e.log_decay)
            weights_of(V0, lambda: e.query(At(Q1), 1), e.tail)
            weights_of(V0 + 1, lambda: e.value(At(V0), 0), e.keys_end)
            weights_of(V0 + 2, lambda: e.value(At(V0 + 1), 1), e.keys_near)
            weights_of(V0 + 3, lambda: e.value(At(V0 + 2), 2), e.queries_near)
            weights_of(R0, lambda: e.value(At(V0 + 3), 3), e.queries_far)
            weights_of(R1, lambda: e.gate(At(R0), 0), lambda: e.scores(At(S)))
            weights_of(R2, lambda: e.gate(At(R1), 1), lambda: e.head_a(At(H0), 0))
            weights_of(R3, lambda: e.head_b(At(H0), 0), lambda: e.gate(At(R2), 2), lambda: e.head_a(At(H1), 1))
            pend = lambda: (e.head_b(At(H1), 1), e.gate(At(R3), 3), e.head_a(At(H2), 2), e.head_a(At(H3), 3),
                            e.head_b(At(H2), 2), e.head_b(At(H3), 3))
            pend = run(eng, split, pend, first_of("gla_out"), 4, [finish(3)] * 2, False)
            pend = ffn(1, pend)
            pend()
            e.norm(4)
            e.final()

        @block.scalar
        def _(act):
            for j in range(4):
                act.dma_start(x_tok[:, :, j * GW:(j + 1) * GW],
                              x.rearrange("(m p) n -> p m n", p=P)[:, :, j * GW:(j + 1) * GW])\
                   .then_inc(x_loaded[j], 16)
                if j == 0:
                    for at, src in ((V_MIX, norm_mix), (V_FFN, norm_ffn), (V_CONV, conv_w)):
                        n = src.shape[0] * DT
                        act.dma_start(rows_a[at:at + n, :], src.rearrange("l (k p) -> (l k) p", p=P))\
                           .then_inc(vectors_loaded, 16)
                    for rows, src in ((rows_a[V_FINAL:V_FINAL + DT, :], norm_final),
                                      (rows_b[0:KEY // P, :], gla_b_gate),
                                      (rows_b[KEY // P:, :], gla_norm)):
                        act.dma_start(rows, src.rearrange("(k p) -> k p", p=P)).then_inc(vectors_loaded, 16)

            def split(g, a, b, turn, stride):
                for n in range(a, b):
                    i, more = sub_number(g, n, turn, stride)
                    if i % 2 == 0:
                        act.wait_ge(raw_loaded[i // 2 % SLOTS], 16 * (i // 2 // SLOTS + 1) + more * 2)
                    if i >= SLOTS:
                        act.wait_ge(sub_done, i - SLOTS + 1 + more)
                    act.activation(w_hi[:, i % SLOTS], raw_view(i), ACT.Copy).then_inc(hi_ready, 1)

            class Readouts:
                def split_x(self, at, tile0, norm):
                    if norm < 4:
                        for t in range(tile0, tile0 + GT):
                            ins = act.activation(xs[:, t, 0:T], xT[:, t, :], ACT.Copy,
                                                 scale=vec[:, GAIN[norm] + t:GAIN[norm] + t + 1])
                        ins.then_inc(s["xs_hi"], 1)
                    act.activation(work[:, :, :], xT[:, tile0:tile0 + GT, :], ACT.Square)\
                       .then_inc(s["squares"], 1)

                def ingest(self, at, j):
                    if j == 0:
                        act.wait_ge(vectors_ready, 2)
                    act.wait_ge(s["half_free"], at.groups_done(1))
                    self.split_x(at, GT * j, 0)

                def finish(self, at, norm):
                    act.wait_ge(s["x_added"], at.value("x_added", 1))
                    self.split_x(at, GT * (FINISH_GROUPS.index(at.g) % 4), norm)

                def partial(self, at):
                    pass

                def norm(self, n):
                    act.wait_ge(ms_ready, n + 1)
                    act.activation(rstd[:, :], rstd[:, :], ACT.Sqrt).then_inc(root_ready, 1)
                    if n == 2:
                        act.wait_ge(gate2_padded, 1)
                        act.dma_start(w_gate2[P - RANK:, :], gla_w_gate2).then_inc(gate2_loaded, 16)

                def conv_c(self, at):
                    pass

                conv_u = conv_c

                def mid_hi(self, at, tiles):
                    act.wait_ge(s["product"], at.value("product", 1))
                    act.activation(mid[:, tiles, 0:T], work[:, :, :], ACT.Copy).then_inc(s["mid_hi"], 1)

                def conv_b(self, at):
                    self.mid_hi(at, mid_tiles(at, first_of("conv_in"), 3))

                def gate(self, at, r=None):
                    act.wait_ge(s["scaled"], at.value("scaled", 1))
                    dst = work[:, :, :] if r is None else r_act[:, GT * r:GT * r + GT, :]
                    act.activation(dst, summed[:, :, :], ACT.Silu).then_inc(s["silu"], 1)

                def up(self, at, phase_first):
                    self.mid_hi(at, mid_tiles(at, phase_first, 2))

                def key(self, at, j):
                    pass

                def zed(self, at):
                    pass

                def query(self, at, j):
                    pass

                def value(self, at, j):
                    pass

                def logits(self, at):
                    act.wait_ge(s["half_free"], at.groups_done(1))
                    act.activation(k_end[:, :, :], cum[:, :, :], ACT.Abs).then_inc(log1p_steps, 1)
                    act.wait_ge(log1p_steps, 1)
                    act.activation(k_end[:, :, :], k_end[:, :, :], ACT.Exp, scale=-1.0).then_inc(log1p_steps, 1)
                    act.wait_ge(log1p_steps, 2)
                    act.activation(k_end[:, :, :], k_end[:, :, :], ACT.Ln, bias=1.0).then_inc(log1p_steps, 1)

                def log_decay(self):
                    act.wait_ge(cum_ready, 1)
                    act.activation(r_act[:, 0:KEY // P, :], cum[:, :, :], ACT.Exp, scale=1.0 / TAU)\
                       .then_inc(exp_cum, 1)
                    act.activation(r_act[:, KEY // P:, :], cum[:, :, :], ACT.Exp, scale=-1.0 / TAU)\
                       .then_inc(exp_cum, 1)

                def tail(self):
                    act.wait_ge(tail_ready, 1)
                    act.activation(k_end[:, :, :], k_end[:, :, :], ACT.Exp, scale=1.0 / TAU).then_inc(tail_exp, 1)

                def keys_end(self):
                    pass

                keys_near = queries_near = queries_far = keys_end

                def scores(self, at):
                    pass

                def head_a(self, at, h):
                    act.wait_ge(head_copied, h + 1)
                    act.activation(work[:, :, :], head_out[:, h % 2], ACT.Square).then_inc(head_squares, 1)

                def head_b(self, at, h):
                    act.wait_ge(s["half_free"], at.groups_done(1))
                    act.activation(q_t[:, HEADS + h, :], q_t[:, HEADS + h, :], ACT.Sqrt).then_inc(head_root, 1)
                    self.mid_hi(at, slice(GT * h, GT * h + GT))

                def final(self):
                    for j in range(4):
                        at = At(first_of("store") + j)
                        act.wait_ge(turned, 4 + j + 1)
                        act.activation(y_tok[:, 0, j * GW:(j + 1) * GW], bank(at.half, 0), ACT.Copy)\
                           .then_inc(y_copied[0], 1)

            whole_program(act, split, Readouts())

        @block.vector
        def _(dve):
            wide_rstd = rstd[:, 0:T].unsqueeze(1).to_broadcast([P, GT, T])
            wide_rstd_sq = rstd_sq[:, :].unsqueeze(1).to_broadcast([P, GT, T])

            def split(g, a, b, turn, stride):
                for n in range(a, b):
                    i, more = sub_number(g, n, turn, stride)
                    dve.wait_ge(hi_ready, i + 1 + more)
                    dve.tensor_tensor(w_lo[:, i % SLOTS], raw_view(i), w_hi[:, i % SLOTS].bitcast(f32),
                                      ALU.subtract).then_inc(lo_ready, 1)

            def add_parts(at, out=None, half=None):
                dve.wait_ge(sub_done, at.subs_done())
                dve.tensor_reduce(summed[:, :, :], two_parts(at.half), AX.X, ALU.add).then_inc(s["half_free"], 1)
                dve.wait_ge(s["half_free"], at.groups_done(1))

            class Readouts:
                def split_x(self, at, tile0, norm):
                    if norm < 4:
                        dve.wait_ge(s["xs_hi"], at.value("xs_hi", 1))
                        for t in range(tile0, tile0 + GT):
                            ins = dve.scalar_tensor_tensor(
                                out=xs[:, t, T:2 * T], in0=xT[:, t, :],
                                scalar=vec[:, GAIN[norm] + t:GAIN[norm] + t + 1],
                                in1=xs[:, t, 0:T].bitcast(f32), op0=ALU.mult, op1=ALU.subtract)
                        ins.then_inc(s["xs_ready"], 1)
                    dve.wait_ge(s["squares"], at.value("squares", 1))
                    out, done = (sum_group, group_summed) if tile0 else (sum_x, s["sumsq"])
                    dve.tensor_reduce(out[:, :], work[:, :, :].rearrange("p a t -> p t a"), AX.X, ALU.add)\
                       .then_inc(done, 1)
                    if tile0:
                        dve.wait_ge(group_summed, 3 * norm + tile0 // GT)
                        dve.wait_ge(s["sumsq"], at.value("sumsq", 0))
                        dve.tensor_tensor(sum_x[:, :], sum_x[:, :], sum_group[:, :], ALU.add)\
                           .then_inc(s["sumsq"], 1)

                def ingest(self, at, j):
                    if j == 0:
                        dve.wait_ge(vectors_turned, 2)
                        dve.tensor_copy(vec[:, 0:P], bank(0, 3)[:, 0:P]).then_inc(vectors_ready, 1)
                        dve.tensor_copy(vec[:, P:], bank(0, 3)[:, P:V_HEAD + DV // P]).then_inc(vectors_ready, 1)
                        dve.wait_ge(vectors_ready, 2)
                    dve.wait_ge(turned, j + 1)
                    dve.tensor_copy(xT[:, GT * j:GT * j + GT, :], packed(at.half, GT)).then_inc(s["half_free"], 1)
                    dve.wait_ge(s["half_free"], at.groups_done(1))
                    self.split_x(at, GT * j, 0)

                def add_residual(self, at, tile0):
                    add_parts(at)
                    dve.tensor_tensor(xT[:, tile0:tile0 + GT, :], xT[:, tile0:tile0 + GT, :], summed[:, :, :],
                                      ALU.add).then_inc(s["x_added"], 1)

                def finish(self, at, norm):
                    tile0 = GT * (FINISH_GROUPS.index(at.g) % 4)
                    self.add_residual(at, tile0)
                    dve.wait_ge(s["x_added"], at.value("x_added", 1))
                    self.split_x(at, tile0, norm)

                def partial(self, at):
                    first = first_of(GROUPS[at.g][2])
                    self.add_residual(at, GT * (at.g - first))

                def norm(self, n):
                    half = (first_of(("conv_in", "ffn0_in0", "gla_in", "ffn1_in0", "store")[n]) + 1) % 2
                    dve.wait_ge(mean_done, n + 1)
                    dve.tensor_scalar(rstd[:, :], bank(half, 0)[:, 0:T + 2], EPS, None, ALU.add)\
                       .then_inc(ms_ready, 1)
                    dve.wait_ge(root_ready, n + 1)
                    dve.reciprocal(rstd[:, :], rstd[:, :]).then_inc(rstd_ready, 1)
                    dve.wait_ge(rstd_ready, n + 1)
                    if n == 2:
                        dve.memset(w_gate2[:, :], 0.0).then_inc(gate2_padded, 1)
                    if n == 0:
                        dve.tensor_tensor(rstd_sq[:, :], rstd[:, 0:T], rstd[:, 0:T], ALU.mult)\
                           .then_inc(rstd_sq_ready, 1)
                        dve.memset(conv_in[:, :, 0:2], 0.0).then_inc(conv_edge, 1)
                        dve.wait_ge(rstd_sq_ready, 1)
                        dve.wait_ge(conv_edge, 1)

                def conv_c(self, at):
                    add_parts(at)
                    dve.tensor_tensor(conv_gate[:, :, :], summed[:, :, :], wide_rstd_sq, ALU.mult)\
                       .then_inc(s["scaled"], 1)

                def conv_u(self, at):
                    j = (at.g - first_of("conv_in")) // 3
                    add_parts(at)
                    dve.wait_ge(s["scaled"], at.value("scaled", 0))
                    dve.tensor_tensor(conv_in[:, :, 2:], summed[:, :, :], conv_gate[:, :, :], ALU.mult)\
                       .then_inc(s["scaled"], 1)
                    dve.wait_ge(s["scaled"], at.value("scaled", 1))
                    for tap in range(3):
                        if tap:
                            dve.wait_ge(s["taps"], at.value("taps", tap))
                        for t in range(GT):
                            col = V_CONV + tap * DT + GT * j + t
                            w = vec[:, col:col + 1]
                            if tap == 0:
                                ins = dve.tensor_scalar(conv_y[:, t, :], conv_in[:, t, 0:T], w, None, ALU.mult)
                            else:
                                ins = dve.scalar_tensor_tensor(out=conv_y[:, t, :], in0=conv_in[:, t, tap:tap + T],
                                                               scalar=w, in1=conv_y[:, t, :],
                                                               op0=ALU.mult, op1=ALU.add)
                        ins.then_inc(s["taps"], 1)

                def split_product(self, at, tiles):
                    dve.wait_ge(s["mid_hi"], at.value("mid_hi", 1))
                    dve.tensor_tensor(mid[:, tiles, T:2 * T], work[:, :, :], mid[:, tiles, 0:T].bitcast(f32),
                                      ALU.subtract).then_inc(s["mid_ready"], 1)

                def conv_b(self, at):
                    add_parts(at)
                    dve.tensor_tensor(summed[:, :, :], summed[:, :, :], wide_rstd, ALU.mult)\
                       .then_inc(s["scaled"], 1)
                    dve.wait_ge(s["scaled"], at.value("scaled", 1))
                    dve.wait_ge(s["taps"], at.value("taps", 0))
                    dve.tensor_tensor(work[:, :, :], summed[:, :, :], conv_y[:, :, :], ALU.mult)\
                       .then_inc(s["product"], 1)
                    self.split_product(at, mid_tiles(at, first_of("conv_in"), 3))

                def gate(self, at, r=None):
                    add_parts(at)
                    dve.tensor_tensor(summed[:, :, :], summed[:, :, :], wide_rstd, ALU.mult)\
                       .then_inc(s["scaled"], 1)
                    if r is not None:
                        dve.wait_ge(s["silu"], at.value("silu", 1))

                def up(self, at, phase_first):
                    dve.wait_ge(s["silu"], at.value("silu", 0))
                    add_parts(at)
                    dve.tensor_tensor(summed[:, :, :], summed[:, :, :], wide_rstd, ALU.mult)\
                       .then_inc(s["scaled"], 1)
                    dve.wait_ge(s["scaled"], at.value("scaled", 1))
                    dve.tensor_tensor(work[:, :, :], work[:, :, :], summed[:, :, :], ALU.mult)\
                       .then_inc(s["product"], 1)
                    self.split_product(at, mid_tiles(at, phase_first, 2))

                def key(self, at, j):
                    add_parts(at)
                    dve.tensor_tensor(k_t[:, GT * j:GT * j + GT, :], summed[:, :, :], wide_rstd, ALU.mult)\
                       .then_inc(s["scaled"], 1)

                def query(self, at, j):
                    add_parts(at)
                    dve.scalar_tensor_tensor(out=q_t[:, GT * j:GT * j + GT, :], in0=summed[:, :, :],
                                             scalar=DK ** -0.5, in1=wide_rstd, op0=ALU.mult, op1=ALU.mult)\
                       .then_inc(s["scaled"], 1)

                def zed(self, at):
                    dve.memset(reset[:, :], 1.0).then_inc(reset_ready, 1)
                    dve.wait_ge(reset_ready, 1)
                    dve.memset(reset[:, 0:T:CHUNK], 0.0).then_inc(reset_ready, 1)
                    dve.wait_ge(sub_done, at.subs_done())
                    dve.tensor_reduce(summed[:, 0, :], bank(at.half, 0).rearrange("p (h t) -> p t h", h=2),
                                      AX.X, ALU.add).then_inc(s["half_free"], 1)
                    dve.wait_ge(s["half_free"], at.groups_done(1))
                    dve.tensor_tensor(zT[:, :], summed[:, 0, :], rstd[:, 0:T], ALU.mult)\
                       .then_inc(s["scaled"], 1)

                def logits(self, at):
                    dve.wait_ge(logits_done, 1)
                    for t in range(KEY // P):
                        ins = dve.tensor_scalar(cum[:, t, :], packed(at.half, 8)[:, t, :],
                                                vec[:, V_BIAS + t:V_BIAS + t + 1], None, ALU.add)
                    ins.then_inc(s["half_free"], 1)

                def log_decay(self):
                    dve.wait_ge(log1p_steps, 3)
                    dve.scalar_tensor_tensor(out=k_end[:, :, :], in0=cum[:, :, :], scalar=0.0, in1=k_end[:, :, :],
                                             op0=ALU.min, op1=ALU.subtract).then_inc(log_decay_ready, 1)
                    dve.wait_ge(log_decay_ready, 1)
                    dve.wait_ge(reset_ready, 2)
                    for t in range(KEY // P):
                        ins = dve.tensor_tensor_scan(cum[:, t, :], reset[:, :], k_end[:, t, :], 0.0,
                                                     ALU.mult, ALU.add)
                    ins.then_inc(cum_ready, 1)

                def tail(self):
                    chunks = cum[:, :, :].rearrange("p a (n c) -> p (a n) c", c=CHUNK)
                    dve.wait_ge(cum_ready, 1)
                    dve.tensor_tensor(k_end[:, :, :].rearrange("p a (n c) -> p (a n) c", c=CHUNK),
                                      chunks[:, :, CHUNK - 1:CHUNK].to_broadcast([P, KEY // P * NCHUNK, CHUNK]),
                                      chunks, ALU.subtract).then_inc(tail_ready, 1)
                    dve.wait_ge(exp_cum, 2)
                    dve.tensor_copy(decay[:, :, :], r_act[:, 0:KEY // P, CHUNK - 1::CHUNK]).then_inc(decay_ready, 1)

                def keys_end(self):
                    dve.wait_ge(tail_exp, 1)
                    dve.tensor_tensor(k_end[:, :, :], k_end[:, :, :], k_t[:, :, :], ALU.mult).then_inc(keys_ready, 1)

                def keys_near(self):
                    dve.tensor_tensor(k_t[:, :, :], k_t[:, :, :], r_act[:, KEY // P:, :], ALU.mult)\
                       .then_inc(keys_ready, 1)

                def queries_near(self):
                    dve.tensor_tensor(q_t[:, :, :], q_t[:, :, :], r_act[:, 0:KEY // P, :], ALU.mult)\
                       .then_inc(q_ready, 1)

                def queries_far(self):
                    def over(n):
                        return decay[:, :, n:n + 1].to_broadcast([P, KEY // P, CHUNK])

                    dve.wait_ge(q_ready, 1)
                    dve.wait_ge(decay_ready, 1)
                    dve.tensor_tensor(q_far[:, :, 0, :], q_t[:, :, 2 * CHUNK:3 * CHUNK], over(1), ALU.mult)\
                       .then_inc(q_far_steps, 1)
                    dve.tensor_tensor(q_far[:, :, 2, :], q_t[:, :, 3 * CHUNK:], over(2), ALU.mult)\
                       .then_inc(q_far_steps, 1)
                    dve.wait_ge(q_far_steps, 2)
                    dve.tensor_tensor(q_far[:, :, 1, :], q_far[:, :, 2, :], over(1), ALU.mult)\
                       .then_inc(q_far_steps, 1)

                def value(self, at, j):
                    dve.wait_ge(sub_done, at.subs_done())
                    for m in range(2):
                        ins = dve.tensor_scalar(v_tok[:, m, j * GW:(j + 1) * GW], bank(at.half, m),
                                                rstd[:, T + m:T + m + 1], None, ALU.mult)
                    ins.then_inc(s["half_free"], 1)

                def scores(self, at):
                    dve.wait_ge(scores_done, 1)
                    banks = ps[:, 4 * at.half:4 * at.half + 4, :]
                    for rows, cols in ((slice(0, CHUNK), slice(0, T)), (slice(CHUNK, P), slice(CHUNK, T)),
                                       (slice(0, CHUNK), slice(T, 3 * P)),
                                       (slice(CHUNK, P), slice(T + CHUNK, 3 * P))):
                        ins = dve.tensor_copy(att[rows, :, cols], banks[rows, :, cols])
                    ins.then_inc(s["half_free"], 1)

                def head_a(self, at, h):
                    dve.wait_ge(head_done, h + 1)
                    dve.tensor_copy(head_out[:, h % 2], packed(at.half, GT)).then_inc(head_copied, 1)
                    dve.wait_ge(head_squares, h + 1)
                    dve.tensor_reduce(q_t[:, h, :], work[:, :, :].rearrange("p a t -> p t a"), AX.X, ALU.add)\
                       .then_inc(head_sumsq, 1)

                def head_b(self, at, h):
                    norm = q_t[:, HEADS + h, :]
                    dve.wait_ge(head_mean, h + 1)
                    dve.tensor_scalar(norm, bank(at.half, 2)[:, 0:T], EPS, None, ALU.add)\
                       .then_inc(s["half_free"], 1)
                    dve.wait_ge(head_root, h + 1)
                    dve.reciprocal(norm, norm).then_inc(head_rstd, 1)
                    dve.wait_ge(head_rstd, h + 1)
                    for e in range(GT):
                        ins = dve.scalar_tensor_tensor(out=work[:, e, :], in0=head_out[:, h % 2, e, :],
                                                       scalar=vec[:, V_HEAD + e:V_HEAD + e + 1], in1=norm,
                                                       op0=ALU.mult, op1=ALU.mult)
                    ins.then_inc(head_scaled, 1)
                    dve.wait_ge(head_scaled, h + 1)
                    dve.tensor_tensor(work[:, :, :], work[:, :, :], r_act[:, GT * h:GT * h + GT, :],
                                      ALU.mult).then_inc(s["product"], 1)
                    self.split_product(at, slice(GT * h, GT * h + GT))

                def final(self):
                    for t in range(DT):
                        ins = dve.scalar_tensor_tensor(out=y_norm[:, t, :], in0=xT[:, t, :],
                                                       scalar=vec[:, V_FINAL + t:V_FINAL + t + 1],
                                                       in1=rstd[:, 0:T], op0=ALU.mult, op1=ALU.mult)
                        if t % GT == GT - 1:
                            ins.then_inc(y_ready, 1)
                    for j in range(4):
                        at = At(first_of("store") + j)
                        dve.wait_ge(turned, 4 + j + 1)
                        dve.tensor_copy(y_tok[:, 1, j * GW:(j + 1) * GW], bank(at.half, 1))\
                           .then_inc(y_copied[1], 1)

            whole_program(dve, split, Readouts())

        @block.tensor
        def _(pe):
            def half_is_free(g, more=0):
                if g >= 2:
                    pe.wait_ge(s["half_free"], g - 1 + more)

            def project(g, operand, ready=None, turn=0, stride=0, before_sub=None, by_token=False):
                subs = GROUPS[g][1]
                half_is_free(g, turn * stride if stride else 0)
                for n in range(subs):
                    if before_sub and before_sub[0] == n:
                        before_sub[1]()
                    i, more = sub_number(g, n, turn, stride)
                    if ready and n % 2 == 0:
                        pe.wait_ge(ready[0], ready[1] + n // 2 + 1)
                    pe.wait_ge(lo_ready, i + 1 + more)
                    for kk in range(SUB_K):
                        k = n * SUB_K + kk
                        start, stop = k == 0, k == subs * SUB_K - 1
                        hi, lo = w_hi[:, i % SLOTS, kk, :], w_lo[:, i % SLOTS, kk, :]
                        if by_token:
                            for m in range(2):
                                x_hi = operand[:, k, m * P:(m + 1) * P]
                                x_lo = operand[:, k, T + m * P:T + (m + 1) * P]
                                pe.matmul(bank(g % 2, m), x_hi, lo, start=start, stop=False)
                                pe.matmul(bank(g % 2, m), x_lo, hi, start=False, stop=False)
                                mm = pe.matmul(bank(g % 2, m), x_hi, hi, start=False, stop=stop)
                        else:
                            for o in range(GT):
                                cols = slice(o * P, (o + 1) * P)
                                pe.matmul(bank(g % 2, o), hi[:, cols], operand[:, k, :], start=start, stop=False)
                                mm = pe.matmul(bank(g % 2, o)[:, T:2 * T], lo[:, cols], operand[:, k, 0:T],
                                               start=False, stop=stop)
                    mm.then_inc(sub_done, 1)

            def mean_square(n, half, gap=None):
                pe.wait_ge(s["sumsq"], 4 * (n + 1))
                pe.matmul(bank(half, 0)[:, 0:T], mean_x[:, :], sum_x[:, :], start=True, stop=True)
                for m in range(2):
                    mm = pe.matmul(bank(half, 0)[:, T + m:T + m + 1], sum_x[:, m * P:(m + 1) * P], mean_x[:, 0:1],
                                   start=True, stop=True)
                mm.then_inc(mean_done, 1)

            def first_group(g, norm):
                project(g, xs, ready=(s["xs_ready"], 4 * norm),
                        before_sub=(6, lambda: mean_square(norm, (g + 1) % 2)))
                pe.wait_ge(ms_ready, norm + 1)

            pe.wait_ge(consts_ready, 4)
            for j in range(4):
                half_is_free(j)
                pe.wait_ge(x_loaded[j], 16)
                for t in range(GT):
                    for m in range(2):
                        mm = pe.transpose(packed(j % 2, GT)[:, t, m * P:(m + 1) * P],
                                          x_tok[:, m, (GT * j + t) * P:(GT * j + t + 1) * P], ident[:, :])
                mm.then_inc(turned, 1)
                if j == 0:
                    pe.wait_ge(vectors_loaded, 6 * 16)
                    pe.transpose(bank(0, 3)[:, 0:P], rows_a[:, :], ident[:, :]).then_inc(vectors_turned, 1)
                    rows = KEY // P + DV // P
                    pe.transpose(bank(0, 3)[:, P:P + rows], rows_b[:, :], ident[0:rows, 0:rows])\
                      .then_inc(vectors_turned, 1)

            g = first_of("conv_in")
            first_group(g, 0)
            project(g + 1, xs)
            with pe.Fori(0, (count_of("conv_in") - 2) // 2) as i:
                for q in range(2):
                    project(g + 2 + q, xs, turn=i, stride=2)
            g = first_of("conv_out")
            with pe.Fori(0, 2) as i:
                for q in range(2):
                    project(g + q, mid, ready=(s["mid_ready"], before("mid_ready", g) - 4), turn=i, stride=2)

            def ffn(layer):
                for n, pairs in enumerate(PIECES):
                    g = first_of(f"ffn{layer}_in{n}")
                    done = 0
                    if n == 0:
                        first_group(g, 2 * layer + 1)
                        project(g + 1, xs)
                        done = 2
                    with pe.Fori(0, pairs - done // 2) as i:
                        for q in range(2):
                            project(g + done + q, xs, turn=i, stride=2)
                    g = first_of(f"ffn{layer}_out{n}")
                    with pe.Fori(0, 2) as i:
                        for q in range(2):
                            project(g + q, mid, ready=(s["mid_ready"], before("mid_ready", g) - pairs),
                                    turn=i, stride=2)

            ffn(0)

            g = first_of("gla_in")
            K0, Z, K1, Y, Q0, Q1, V0, R0, S = g, g + 1, g + 2, g + 3, g + 4, g + 5, g + 6, g + 10, g + 11
            R1, H0, R2, H1, R3, H2, H3 = range(g + 12, g + 19)
            first_group(K0, 2)
            half_is_free(Z)
            for n in range(2):
                i = sub_before(Z) + n
                pe.wait_ge(lo_ready, i + 1)
                hi = w_hi[:, i % SLOTS].rearrange("p a n -> p (a n)").rearrange("p (k n) -> p k n", n=P)
                lo = w_lo[:, i % SLOTS].rearrange("p a n -> p (a n)").rearrange("p (k n) -> p k n", n=P)
                for kk in range(DT // 2):
                    k = n * DT // 2 + kk
                    pe.matmul(bank(Z % 2, 0), hi[:, kk, :], xs[:, k, :], start=k == 0, stop=False)
                    mm = pe.matmul(bank(Z % 2, 0)[:, T:2 * T], lo[:, kk, :], xs[:, k, 0:T], start=False,
                                   stop=k == DT - 1)
                mm.then_inc(sub_done, 1)
            project(K1, xs)
            half_is_free(Y)
            pe.wait_ge(s["scaled"], before("scaled", Z) + 1)
            pe.wait_ge(gate2_loaded, 16)
            for t in range(KEY // P):
                mm = pe.matmul(packed(Y % 2, 8)[:, t, :], w_gate2[:, t * P:(t + 1) * P], zT[:, :],
                               start=True, stop=True)
            mm.then_inc(logits_done, 1)
            project(Q0, xs)
            project(Q1, xs)
            for j in range(4):
                project(V0 + j, xs, by_token=True)
            project(R0, xs)

            half_is_free(S)
            pe.wait_ge(keys_ready, 2)
            pe.wait_ge(q_far_steps, 3)
            for h in range(HEADS):
                for m in range(NCHUNK):
                    keys = slice(m * CHUNK, (m + 1) * CHUNK)
                    rows = slice(CHUNK * (m % 2), CHUNK * (m % 2) + CHUNK)
                    base = T - P if m >= 2 else 0
                    jobs = [(k_t, m, lambda d, m=m: q_t[:, d, m * CHUNK:(m + 1) * CHUNK], 1)]
                    if m + 1 < NCHUNK:
                        jobs.append((k_end, m + 1, lambda d, m=m: q_t[:, d, (m + 1) * CHUNK:(m + 2) * CHUNK], 1))
                    if m == 0:
                        jobs.append((k_end, 2, lambda d: q_far[:, d, 0:2, :].rearrange("p a c -> p (a c)"), 2))
                    if m == 1:
                        jobs.append((k_end, 3, lambda d: q_far[:, d, 2, :], 1))
                    for src, c, query, width in jobs:
                        dst = bank(S % 2, h)[rows, base + c * CHUNK:base + (c + width) * CHUNK]
                        for half in range(2):
                            d = 2 * h + half
                            mm = pe.matmul(dst, src[:, d, keys], query(d), start=half == 0, stop=half == 1)
            mm.then_inc(scores_done, 1)

            def head(g, h):
                half_is_free(g)
                if h == 0:
                    pe.wait_ge(att_masked, 2)
                for e in range(GT):
                    cols = slice(h * DV + e * P, h * DV + (e + 1) * P)
                    dst = packed(g % 2, GT)[:, e, :]
                    pe.matmul(dst, v_tok[:, 0, cols], att[:, h, 0:T], start=True, stop=False)
                    mm = pe.matmul(dst[:, P:T], v_tok[:, 1, cols], att[:, h, T:3 * P], start=False, stop=True)
                mm.then_inc(head_done, 1)

            def head_mean_square(g, h):
                pe.wait_ge(head_sumsq, h + 1)
                pe.matmul(bank(g % 2, 2)[:, 0:T], mean_head[:, :], q_t[:, h, :], start=True, stop=True)\
                  .then_inc(head_mean, 1)

            project(R1, xs)
            head(H0, 0)
            project(R2, xs, before_sub=(6, lambda: head_mean_square(H0, 0)))
            head(H1, 1)
            project(R3, xs, before_sub=(6, lambda: head_mean_square(H1, 1)))
            head(H2, 2)
            head(H3, 3)
            head_mean_square(H2, 2)
            head_mean_square(H3, 3)
            g = first_of("gla_out")
            with pe.Fori(0, 2) as i:
                for q in range(2):
                    project(g + q, mid, ready=(s["mid_ready"], before("mid_ready", g) - 4), turn=i, stride=2)
            ffn(1)

            g = first_of("store")
            mean_square(4, (g + 1) % 2)
            for j in range(4):
                half = (g + j) % 2
                pe.wait_ge(y_ready, j + 1)
                if j >= 2:
                    pe.wait_ge(y_copied[0], j - 1)
                    pe.wait_ge(y_copied[1], j - 1)
                for m in range(2):
                    for t in range(GT):
                        mm = pe.transpose(bank(half, m)[:, t * P:(t + 1) * P],
                                          y_norm[:, GT * j + t, m * P:(m + 1) * P], ident[:, :])
                mm.then_inc(turned, 1)


def kernel(**inputs):
    import numpy as np
    import concourse.bacc as bacc
    from concourse.bass_utils import run_bass_kernel_spmd

    shapes = {
        "x": (T, D), "norm_mix": (2, D), "norm_ffn": (2, D), "norm_final": (D,), "conv_w_in": (D, 3 * D),
        "conv_w": (3, D), "conv_w_out": (D, D), "gla_w_in": (D, GLA_COLS), "gla_w_gate2": (RANK, KEY),
        "gla_b_gate": (KEY,), "gla_norm": (DV,), "gla_w_out": (D, D), "ffn_w_in": (2, D, 2 * F),
        "ffn_w_out": (2, F, D),
    }
    nc = bacc.Bacc("TRN2", target_bir_lowering=False, num_devices=1)
    arrays, args = {}, []
    for name, shape in shapes.items():
        a = np.ascontiguousarray(inputs[name]).reshape(shape)
        arrays[f"in_{name}"] = a
        args.append(nc.dram_tensor(f"in_{name}", shape, mybir.dt.from_np(a.dtype), kind="ExternalInput").ap())
    args.append(nc.dram_tensor("trunk_out", (T, D), mybir.dt.float32, kind="ExternalOutput").ap())
    trunk(nc, *args)
    r = run_bass_kernel_spmd(nc, [arrays], core_ids=[0])
    return r.results[0]["trunk_out"].reshape(1, T, D)
```

```python
import concourse.bass as bass
from concourse import mybir
from contextlib import ExitStack


P = 128
T = 256
D = 2048
DT = D // P
GW = 512
GT = GW // P
F = 5632
PAIRS = F // GW
PIECES = (4, 4, 3)
HEADS, DK, DV, CHUNK, RANK = 4, 256, 512, 64, 16
KEY = HEADS * DK
NCHUNK = T // CHUNK
GLA_COLS = 2 * KEY + 2 * D + RANK
EPS = 1e-6
TAU = 16.0
SLOTS = 4
SUB_K = 2
MEAN_SUB = 6

V_MIX, V_FFN, V_FINAL, V_CONV, V_BIAS, V_HEAD = 0, 2 * DT, 4 * DT, 5 * DT, 8 * DT, 8 * DT + KEY // P

ADDS = {
    "ingest": dict(half_free=1, xs_hi=1, squares=1, xs_ready=1, sumsq=1),
    "partial": dict(half_free=1, x_added=1),
    "finish": dict(half_free=1, x_added=1, xs_hi=1, squares=1, xs_ready=1, sumsq=1),
    "conv_c": dict(half_free=1, scaled=1),
    "conv_u": dict(half_free=1, scaled=1, taps=3),
    "conv_b": dict(half_free=1, scaled=1, product=1, mid_hi=1, mid_ready=1),
    "gate": dict(half_free=1, scaled=1, silu=1),
    "up": dict(half_free=1, scaled=1, product=1, mid_hi=1, mid_ready=1),
    "key": dict(half_free=1, scaled=1),
    "query": dict(half_free=1, scaled=1),
    "zed": dict(half_free=1, scaled=1),
    "logits": dict(half_free=1),
    "value": dict(half_free=1),
    "scores": dict(half_free=1),
    "head": dict(half_free=1, product=1, mid_hi=1, mid_ready=1),
    "store": dict(half_free=1),
}
NO_WEIGHTS = ("ingest", "logits", "scores", "head", "store")


def schedule():
    groups = [("ingest", 0, "ingest")] * 4
    groups += [("conv_c", 8, "conv_in"), ("conv_u", 8, "conv_in"), ("conv_b", 8, "conv_in")] * 4
    groups += [("finish", 8, "conv_out")] * 4

    def ffn(layer):
        out = []
        for n, pairs in enumerate(PIECES):
            out += [("gate", 8, f"ffn{layer}_in{n}"), ("up", 8, f"ffn{layer}_in{n}")] * pairs
            kind = "finish" if n == len(PIECES) - 1 else "partial"
            out += [(kind, 2 * pairs, f"ffn{layer}_out{n}")] * 4
        return out

    groups += ffn(0)
    for kind in ("key", "zed", "key", "logits", "query", "query", "value", "value", "value", "value",
                 "gate", "scores", "gate", "head", "head", "gate", "head", "head", "gate"):
        groups.append((kind, 0 if kind in NO_WEIGHTS else 2 if kind == "zed" else 8, "gla_in"))
    groups += [("finish", 8, "gla_out")] * 4
    groups += ffn(1)
    groups += [("store", 0, "store")] * 4
    return groups


GROUPS = schedule()


def first_of(phase):
    return [p for _, _, p in GROUPS].index(phase)


def count_of(phase):
    return sum(p == phase for _, _, p in GROUPS)


def sub_before(g):
    return sum(s for _, s, _ in GROUPS[:g])


def before(name, g):
    return sum(ADDS[k].get(name, 0) for k, _, _ in GROUPS[:g])


class At:

    def __init__(self, g, turn=0, cycle=0):
        self.g, self.turn, self.cycle = g, turn, cycle
        self.half = g % 2

    def value(self, name, more):
        step = before(name, self.g + self.cycle) - before(name, self.g)
        return before(name, self.g) + more + (self.turn * step if self.cycle else 0)

    def subs_done(self):
        step = sub_before(self.g + self.cycle) - sub_before(self.g)
        return sub_before(self.g + 1) + (self.turn * step if self.cycle else 0)

    def groups_done(self, more):
        return self.g + more + (self.turn * self.cycle if self.cycle else 0)


def trunk(nc, x, norm_mix, norm_ffn, norm_final, conv_w_in, conv_w, conv_w_out, gla_w_in, gla_w_gate2,
          gla_b_gate, gla_norm, gla_w_out, ffn_w_in, ffn_w_out, out):
    f32, f32r = mybir.dt.float32, mybir.dt.float32r
    ACT, ALU, AX = mybir.ActivationFunctionType, mybir.AluOpType, mybir.AxisListType
    ctx = ExitStack()
    with ctx:
        def sb(name, shape, dt=f32, where=None):
            return (where or ctx).enter_context(nc.sbuf_tensor(name, shape, dt))

        def sem(name):
            return ctx.enter_context(nc.semaphore(name))

        xT = sb("xT", [P, DT, T])
        xs = sb("xs", [P, DT, 2 * T], f32r)
        raw = sb("raw", [P, SLOTS, 4, GW])
        w_hi = sb("w_hi", [P, SLOTS, SUB_K, GW], f32r)
        w_lo = sb("w_lo", [P, SLOTS, SUB_K, GW], f32r)
        summed = sb("summed", [P, GT, T])
        work = sb("work", [P, GT, T])
        sum_x = sb("sum_x", [P, T])
        sum_group = sb("sum_group", [P, T])
        rstd = sb("rstd", [P, T + 2])
        rstd_sq = sb("rstd_sq", [P, T])
        vec = sb("vec", [P, V_HEAD + DV // P])
        ident = sb("ident", [P, P])
        mean_x = sb("mean_x", [P, P])
        mean_head = sb("mean_head", [P, P])

        with ExitStack() as use:
            q_far = sb("q_far", [P, KEY // P, 3, CHUNK], where=use)
            w_gate2 = sb("w_gate2", [P, KEY], where=use)
            zT = sb("zT", [P, T], where=use)
            decay = sb("decay", [P, KEY // P, NCHUNK], where=use)
            reset = sb("reset", [P, T], where=use)
            pad_words = (DT * T - KEY // P * 3 * CHUNK - KEY - T - KEY // P * NCHUNK - T)
            sb("unused", [P, pad_words], where=use)
            r_act = sb("r_act", [P, DT, T], where=use)
        mid = sb("mid", [P, DT, 2 * T], f32r)

        with ExitStack() as use:
            x_tok = sb("x_tok", [P, 2, D], where=use)
            rows_a = sb("rows_a", [P, P], where=use)
            rows_b = sb("rows_b", [KEY // P + DV // P, P], where=use)
        with ExitStack() as use:
            conv_gate = sb("conv_gate", [P, GT, T], where=use)
            conv_in = sb("conv_in", [P, GT, T + 2], where=use)
            conv_y = sb("conv_y", [P, GT, T], where=use)
        with ExitStack() as use:
            y_norm = sb("y_norm", [P, DT, T], where=use)
            y_tok = sb("y_tok", [P, 2, D], where=use)
        cum = sb("cum", [P, KEY // P, T])
        q_t = sb("q_t", [P, KEY // P, T])
        k_t = sb("k_t", [P, KEY // P, T])
        k_end = sb("k_end", [P, KEY // P, T])
        v_tok = sb("v_tok", [P, 2, D])
        head_out = [buf[:, GT * a:GT * a + GT, :] for buf in (k_t, k_end) for a in range(2)]
        att = cum[:, :, :].rearrange("p a t -> p (a t)")[:, 0:HEADS * 3 * P].rearrange("p (h c) -> p h c", h=HEADS)

        ps = ctx.enter_context(nc.psum_tensor("ps", [P, 8, GW], f32))

        raw_loaded = [sem(f"raw_loaded{i}") for i in range(SLOTS)]
        hi_ready = sem("hi_ready")
        lo_ready = sem("lo_ready")
        sub_done = sem("sub_done")
        x_loaded = [sem(f"x_loaded{j}") for j in range(4)]
        rows_a_loaded = sem("rows_a_loaded")
        rows_b_loaded = sem("rows_b_loaded")
        gate2_loaded = sem("gate2_loaded")
        consts_ready = sem("consts_ready")
        vectors_turned = sem("vectors_turned")
        vectors_ready = sem("vectors_ready")
        turned = sem("turned")
        s = {n: sem(n) for n in ("half_free", "x_added", "xs_hi", "squares", "xs_ready", "sumsq", "scaled",
                                 "taps", "product", "mid_hi", "mid_ready", "silu")}
        group_summed = sem("group_summed")
        mean_done = sem("mean_done")
        ms_ready = sem("ms_ready")
        root_ready = sem("root_ready")
        rstd_ready = sem("rstd_ready")
        rstd_sq_ready = sem("rstd_sq_ready")
        conv_edge = sem("conv_edge")
        zed_done = sem("zed_done")
        gate2_padded = sem("gate2_padded")
        reset_ready = sem("reset_ready")
        logits_done = sem("logits_done")
        log1p_steps = sem("log1p_steps")
        log_decay_ready = sem("log_decay_ready")
        cum_ready = sem("cum_ready")
        exp_cum = sem("exp_cum")
        tail_ready = sem("tail_ready")
        tail_exp = sem("tail_exp")
        decay_ready = sem("decay_ready")
        keys_ready = sem("keys_ready")
        q_ready = sem("q_ready")
        q_far_steps = sem("q_far_steps")
        scores_done = sem("scores_done")
        att_masked = sem("att_masked")
        head_done = sem("head_done")
        head_squares = sem("head_squares")
        head_sumsq = sem("head_sumsq")
        head_mean = sem("head_mean")
        head_ms = sem("head_ms")
        head_root = sem("head_root")
        head_rstd = sem("head_rstd")
        head_scaled = sem("head_scaled")
        y_ready = sem("y_ready")
        y_copied = [sem("y_copied0"), sem("y_copied1")]
        stored = sem("stored")

        def bank(half, b):
            return ps[:, 4 * half + b, :]

        def two_parts(half):
            return ps[:, 4 * half:4 * half + 4, :].rearrange("p b (h t) -> p b t h", h=2)

        def packed(half, tiles):
            return ps[:, 4 * half:4 * half + tiles // 2, :].rearrange("p b (a t) -> p (b a) t", a=2)

        GAIN = [V_MIX, V_FFN, V_MIX + DT, V_FFN + DT, V_FINAL]
        R_GROUPS = [g for g, (k, _, p) in enumerate(GROUPS) if k == "gate" and p == "gla_in"]
        HEAD_GROUPS = [g for g, (k, _, _) in enumerate(GROUPS) if k == "head"]
        Y_READ = [k for k, _, _ in GROUPS].index("logits") + 1
        head_sq = [work[:, :, :], r_act[:, DT - GT:DT, :]]

        def x_turned(j):
            return ps[:, 4 + 2 * (j % 2):6 + 2 * (j % 2), :].rearrange("p b (a t) -> p (b a) t", a=2)

        def head_norm(pair):
            return q_t[:, HEADS + 2 * pair:HEADS + 2 * pair + 2, :]

        FINISH_GROUPS = [g for g, (k, _, _) in enumerate(GROUPS) if k in ("ingest", "finish")]

        block = ctx.enter_context(nc.Block())

        @block.sync
        def _(sp):
            def chunk(c, src, turn=0, step=0, view=None):
                slot = c % SLOTS
                if c >= SLOTS or step:
                    sp.wait_ge(lo_ready, 2 * (c - SLOTS) + 2 + (turn * (2 * step) if step else 0))
                dst = raw[:, slot] if view is None else raw[:, slot].rearrange("p a n -> p (a n)")\
                    .rearrange("p (k n) -> p k n", n=view)
                sp.dma_start(dst, src).then_inc(raw_loaded[slot], 16)

            def matrix(w):
                return w.rearrange("(k p) n -> p k n", p=P)

            def group(c, w, k0, kn, col, turn=0, step=0):
                for n in range(kn // 4):
                    chunk(c + n, w[:, k0 + 4 * n:k0 + 4 * n + 4, bass.ds(col, GW)], turn, step)
                return c + kn // 4

            def x_columns(j):
                sp.dma_start(x_tok[:, :, j * GW:(j + 1) * GW],
                             x.rearrange("(m p) n -> p m n", p=P)[:, :, j * GW:(j + 1) * GW])\
                  .then_inc(x_loaded[j], 16)

            w = matrix(conv_w_in)
            x_columns(0)
            for row, src in ((V_MIX, norm_mix), (V_FFN, norm_ffn), (V_CONV, conv_w)):
                n = src.shape[0] * DT
                sp.dma_start(rows_a[row:row + n, :], src.rearrange("l (k p) -> (l k) p", p=P))\
                  .then_inc(rows_a_loaded, 16)
            sp.dma_start(rows_a[V_FINAL:V_FINAL + DT, :], norm_final.rearrange("(k p) -> k p", p=P))\
              .then_inc(rows_a_loaded, 16)
            x_columns(1)
            for j in range(4):
                chunk(j, w[:, 4 * j:4 * j + 4, D:D + GW])
                if j < 2:
                    x_columns(2 + j)
            c = 4
            for part in (2, 0):
                c = group(c, w, 0, DT, part * D)
            with sp.Fori(0, D // GW - 1) as i:
                for n, part in enumerate((1, 2, 0)):
                    group(c + 4 * n, w, 0, DT, i * GW + (part * D + GW), i, 12)
            c += 12 * (D // GW - 1)
            with sp.Fori(0, D // GW) as i:
                group(c, matrix(conv_w_out), 0, DT, i * GW, i, 4)
            c += 4 * (D // GW)

            def ffn(c, layer):
                w_in, w_out = matrix(ffn_w_in[layer]), matrix(ffn_w_out[layer])
                k0 = 0
                for pairs in PIECES:
                    with sp.Fori(0, pairs) as i:
                        group(c, w_in, 0, DT, i * GW + k0 * P, i, 8)
                        group(c + 4, w_in, 0, DT, i * GW + (F + k0 * P), i, 8)
                    c += 8 * pairs
                    if pairs == SLOTS:
                        with sp.Fori(0, D // GW) as i:
                            group(c, w_out, k0, 4 * pairs, i * GW, i, pairs)
                        c += pairs * (D // GW)
                    else:
                        for n in range(D // GW):
                            c = group(c, w_out, k0, 4 * pairs, n * GW)
                    k0 += 4 * pairs
                return c

            c = ffn(c, 0)
            w = matrix(gla_w_in)
            c = group(c, w, 0, DT, KEY)
            chunk(c, w[:, :, GLA_COLS - P:GLA_COLS], view=P)
            c = group(c + 1, w, 0, DT, KEY + GW)
            for col in (0, GW):
                c = group(c, w, 0, DT, col)
            with sp.Fori(0, 2 * D // GW) as i:
                group(c, w, 0, DT, i * GW + 2 * KEY, i, 4)
            c += 4 * (2 * D // GW)
            with sp.Fori(0, D // GW) as i:
                group(c, matrix(gla_w_out), 0, DT, i * GW, i, 4)
            c += 4 * (D // GW)
            ffn(c, 1)
            for j in range(4):
                sp.wait_ge(y_copied[0], j + 1)
                sp.wait_ge(y_copied[1], j + 1)
                sp.dma_start(out.rearrange("(m p) n -> p m n", p=P)[:, :, j * GW:(j + 1) * GW],
                             y_tok[:, :, j * GW:(j + 1) * GW]).then_inc(stored, 16)
            sp.wait_ge(stored, 4 * 16)

        @block.gpsimd
        def _(pool):
            pool.memset(ident[:, :], 0.0).then_inc(consts_ready, 1)
            pool.memset(mean_x[:, :], 1.0 / D).then_inc(consts_ready, 1)
            pool.memset(mean_head[:, :], 1.0 / DV).then_inc(consts_ready, 1)
            pool.wait_ge(consts_ready, 3)
            pool.affine_select(out=ident[:, :], in_=ident[:, :], compare_op=ALU.not_equal, fill=1.0, base=0,
                               pattern=[[-1, P]], channel_multiplier=1).then_inc(consts_ready, 1)
            pool.wait_ge(s["half_free"], first_of("gla_in") + 12)
            pool.affine_select(out=att[:, :, 0:T], in_=att[:, :, 0:T], compare_op=ALU.is_ge, fill=0.0, base=0,
                               pattern=[[0, HEADS], [1, T]], channel_multiplier=-1).then_inc(att_masked, 1)
            pool.affine_select(out=att[:, :, T:3 * P], in_=att[:, :, T:3 * P], compare_op=ALU.is_ge, fill=0.0,
                               base=0, pattern=[[0, HEADS], [1, P]], channel_multiplier=-1).then_inc(att_masked, 1)

        def one(split, g, slots, turn=0, stride=0):
            subs = GROUPS[g][1]
            early = min(SLOTS - 1, subs) if -1 in slots else min(SLOTS, subs)
            split(g, 0, early, turn, stride)
            for step in slots.get(-1, ()):
                step()
            split(g, early, min(SLOTS, subs), turn, stride)
            for n in range(5):
                for step in slots.get(n, ()):
                    step()
                if SLOTS + n < subs:
                    split(g, SLOTS + n, SLOTS + n + 1, turn, stride)

        def run(eng, split, pending, g0, n, readouts, looped, after_first=None, first_done=False):
            cycle = len(readouts)
            turns = n // cycle
            if not first_done:
                one(split, g0, pending)
            if after_first:
                after_first()
            if looped:
                with eng.Fori(0, turns - 1) as i:
                    for q in range(1, cycle + 1):
                        one(split, g0 + q, readouts[q - 1](At(g0 + q - 1, i, cycle)), i, cycle)
            else:
                for q in range(1, (turns - 1) * cycle + 1):
                    one(split, g0 + q, readouts[(q - 1) % cycle](At(g0 + q - 1)))
            last = g0 + (turns - 1) * cycle
            for q in range(1, cycle):
                one(split, last + q, readouts[q - 1](At(last + q - 1)))
            return readouts[cycle - 1](At(last + cycle - 1))

        def sub_number(g, n, turn, stride):
            return sub_before(g) + n, turn * (sub_before(g + stride) - sub_before(g)) if stride else 0

        def raw_view(i):
            return raw[:, i // 2 % SLOTS, SUB_K * (i % 2):SUB_K * (i % 2) + SUB_K, :]

        def mid_tiles(at, phase_first, per):
            t0 = (at.g - phase_first) // per * GT
            if at.cycle:
                return bass.ds(at.turn * (at.cycle // per * GT) + t0, GT)
            return slice(t0, t0 + GT)

        class Steps:

            def ingest_x(self, at, j): pass
            def add_x(self, at, tile0): pass
            def split_x(self, at, tile0, norm): pass
            def square_x(self, at, tile0, norm): pass
            def norm(self, n): pass
            def conv_c(self, at): pass
            def conv_u(self, at): pass
            def conv_tap(self, at, tap): pass
            def conv_b(self, at): pass
            def split_mid(self, at, tiles): pass
            def normed(self, at, r=None): pass
            def silu(self, at, r=None): pass
            def up(self, at): pass
            def key(self, at, j): pass
            def zed(self, at): pass
            def load_gate2(self): pass
            def logits(self, at): pass
            def log1p(self, n): pass
            def query(self, at, j): pass
            def log_decay(self): pass
            def running_sum(self, tiles): pass
            def exp_cum(self, n): pass
            def tail(self): pass
            def tail_exp(self): pass
            def value(self, at, j): pass
            def keys_end(self): pass
            def keys_near(self): pass
            def queries_near(self): pass
            def queries_far(self): pass
            def scores(self, at): pass
            def head_copy(self, at, h): pass
            def head_square(self, h): pass
            def head_sumsq(self, h): pass
            def head_root(self, pair, at): pass
            def head_rstd(self, pair): pass
            def head_scaled(self, h): pass
            def head_product(self, at, h): pass
            def final(self): pass

        def whole_program(eng, split, e):
            def finish(norm):
                def readout(at):
                    tile0 = GT * (FINISH_GROUPS.index(at.g) % 4)
                    return {0: [lambda: e.add_x(at, tile0)], 2: [lambda: e.split_x(at, tile0, norm)],
                            3: [lambda: e.square_x(at, tile0, norm)]}
                return readout

            def partial(at):
                return {0: [lambda: e.add_x(at, GT * (at.g - first_of(GROUPS[at.g][2])))]}

            def conv_c(at):
                return {0: [lambda: e.conv_c(at)]}

            def conv_u(at):
                return {0: [lambda: e.conv_u(at)]} | {1 + k: [lambda k=k: e.conv_tap(at, k)] for k in range(3)}

            def conv_b(at):
                return {0: [lambda: e.conv_b(at)],
                        2: [lambda: e.split_mid(at, mid_tiles(at, first_of("conv_in"), 3))]}

            def gate(at):
                return {0: [lambda: e.normed(at)], 2: [lambda: e.silu(at)]}

            def up_of(first):
                return lambda at: {0: [lambda: e.up(at)], 2: [lambda: e.split_mid(at, mid_tiles(at, first, 2))]}

            g = first_of("conv_in")
            e.ingest_x(At(0), 0)
            e.ingest_x(At(1), 1)
            for j in range(4):
                if j >= 2:
                    e.ingest_x(At(j), j)
                e.split_x(At(j), GT * j, 0)
                split(g, 2 * j, 2 * j + 2, 0, 0)
                e.square_x(At(j), GT * j, 0)
            pend = run(eng, split, None, g, 12, [conv_c, conv_u, conv_b], False, lambda: e.norm(0), first_done=True)
            pend = run(eng, split, pend, first_of("conv_out"), 4, [finish(1)], False)

            def ffn(layer, pend):
                for n, pairs in enumerate(PIECES):
                    g = first_of(f"ffn{layer}_in{n}")
                    pend = run(eng, split, pend, g, 2 * pairs, [gate, up_of(g)], True,
                               (lambda: e.norm(2 * layer + 1)) if n == 0 else None)
                    last = n == len(PIECES) - 1
                    pend = run(eng, split, pend, first_of(f"ffn{layer}_out{n}"), 4,
                               [finish(2 * layer + 2) if last else partial], False)
                return pend

            pend = ffn(0, pend)
            K0, Z, K1, Y, Q0, Q1, V0, V1, V2, V3, R0, S, R1, H0, H1, R2, H2, H3, R3 = \
                range(first_of("gla_in"), first_of("gla_out"))

            def weights_of(group, slots):
                one(split, group, slots)

            def each(*steps):
                return [(lambda f=f, a=a: f(*a)) for f, *a in steps]

            weights_of(K0, pend)
            e.norm(2)
            weights_of(Z, {0: each((e.key, At(K0), 0), (e.load_gate2,))})
            weights_of(K1, {0: each((e.zed, At(Z)))})
            weights_of(Q0, {-1: each((e.key, At(K1), 1)), 2: each((e.logits, At(Y)), (e.log1p, 0)),
                            3: each((e.log1p, 1)), 4: each((e.log1p, 2))})
            weights_of(Q1, {0: each((e.query, At(Q0), 0)), 1: each((e.log_decay,)),
                            2: each((e.running_sum, range(0, 4))), 3: each((e.running_sum, range(4, 8))),
                            4: each((e.exp_cum, 0))})
            weights_of(V0, {0: each((e.query, At(Q1), 1)), 1: each((e.tail,), (e.exp_cum, 1)),
                            3: each((e.tail_exp,))})
            weights_of(V1, {0: each((e.value, At(V0), 0)), 1: each((e.keys_end,)), 3: each((e.keys_near,))})
            weights_of(V2, {0: each((e.value, At(V1), 1)), 1: each((e.queries_near,)), 3: each((e.queries_far,))})
            weights_of(V3, {0: each((e.value, At(V2), 2))})
            weights_of(R0, {0: each((e.value, At(V3), 3))})
            weights_of(R1, {0: each((e.normed, At(R0), 0), (e.scores, At(S))), 2: each((e.silu, At(R0), 0))})
            weights_of(R2, {-1: each((e.normed, At(R1), 1)), 0: each((e.head_copy, At(H0), 0), (e.head_copy, At(H1), 1)),
                            1: each((e.head_square, 0), (e.head_square, 1), (e.silu, At(R1), 1)),
                            2: each((e.head_sumsq, 0), (e.head_sumsq, 1)),
                            4: each((e.head_root, 0, At(H1)))})
            weights_of(R3, {-1: each((e.normed, At(R2), 2)), 0: each((e.head_copy, At(H2), 2), (e.head_copy, At(H3), 3),
                                    (e.head_square, 2), (e.head_square, 3)),
                            1: each((e.head_sumsq, 2), (e.head_sumsq, 3), (e.silu, At(R2), 2)),
                            2: each((e.head_rstd, 0), (e.head_scaled, 0), (e.head_product, At(H0), 0)),
                            3: each((e.split_mid, At(H0), slice(0, GT)), (e.head_scaled, 1),
                                    (e.head_product, At(H1), 1)),
                            4: each((e.split_mid, At(H1), slice(GT, 2 * GT)), (e.head_root, 1, At(H3)),
                                    (e.head_rstd, 1))})
            pend = {0: each((e.head_scaled, 2), (e.head_product, At(H2), 2),
                            (e.split_mid, At(H2), slice(2 * GT, 3 * GT)), (e.normed, At(R3), 3), (e.silu, At(R3), 3)),
                    1: each((e.head_scaled, 3), (e.head_product, At(H3), 3)),
                    2: each((e.split_mid, At(H3), slice(3 * GT, 4 * GT)))}
            pend = run(eng, split, pend, first_of("gla_out"), 4, [finish(3)], False)
            pend = ffn(1, pend)
            for n in sorted(pend):
                for step in pend[n]:
                    step()
            e.norm(4)
            e.final()

        @block.scalar
        def _(act):
            act.wait_ge(consts_ready, 3)
            act.activation(sum_group[:, 0:P], mean_x[:, :], ACT.Copy)
            act.dma_start(rows_b[0:KEY // P, :], gla_b_gate.rearrange("(k p) -> k p", p=P))\
               .then_inc(rows_b_loaded, 16)
            act.dma_start(rows_b[KEY // P:, :], gla_norm.rearrange("(k p) -> k p", p=P)).then_inc(rows_b_loaded, 16)

            def split(g, a, b, turn, stride):
                for n in range(a, b):
                    i, more = sub_number(g, n, turn, stride)
                    if i % 2 == 0:
                        act.wait_ge(raw_loaded[i // 2 % SLOTS], 16 * (i // 2 // SLOTS + 1) + more * 2)
                    if i >= SLOTS:
                        act.wait_ge(sub_done, i - SLOTS + 1 + more)
                    act.activation(w_hi[:, i % SLOTS], raw_view(i), ACT.Copy).then_inc(hi_ready, 1)

            class Scalar(Steps):
                def split_x(self, at, tile0, norm):
                    if norm < 4:
                        if GROUPS[at.g][0] == "finish":
                            act.wait_ge(s["x_added"], at.value("x_added", 1))
                        else:
                            if at.g == 0:
                                act.wait_ge(vectors_ready, 1)
                            act.wait_ge(s["half_free"], at.groups_done(1))
                        for t in range(tile0, tile0 + GT):
                            ins = act.activation(xs[:, t, 0:T], xT[:, t, :], ACT.Copy,
                                                 scale=vec[:, GAIN[norm] + t:GAIN[norm] + t + 1])
                        ins.then_inc(s["xs_hi"], 1)

                def square_x(self, at, tile0, norm):
                    if norm == 4:
                        act.wait_ge(s["x_added"], at.value("x_added", 1))
                    if at.value("sumsq", 0):
                        act.wait_ge(s["sumsq"], at.value("sumsq", 0))
                    act.activation(work[:, :, :], xT[:, tile0:tile0 + GT, :], ACT.Square)\
                       .then_inc(s["squares"], 1)

                def norm(self, n):
                    act.wait_ge(ms_ready, n + 1)
                    act.activation(rstd[:, :], rstd[:, :], ACT.Sqrt).then_inc(root_ready, 1)

                def load_gate2(self):
                    act.wait_ge(gate2_padded, 1)
                    act.dma_start(w_gate2[P - RANK:, :], gla_w_gate2).then_inc(gate2_loaded, 16)

                def split_mid(self, at, tiles):
                    act.wait_ge(s["product"], at.value("product", 1))
                    act.activation(mid[:, tiles, 0:T], work[:, :, :], ACT.Copy).then_inc(s["mid_hi"], 1)

                def silu(self, at, r=None):
                    act.wait_ge(s["scaled"], at.value("scaled", 1))
                    dst = work[:, :, :] if r is None else r_act[:, GT * r:GT * r + GT, :]
                    act.activation(dst, summed[:, :, :], ACT.Silu).then_inc(s["silu"], 1)

                def log1p(self, n):
                    if n == 0:
                        act.wait_ge(s["half_free"], Y_READ)
                        act.activation(k_end[:, :, :], cum[:, :, :], ACT.Abs).then_inc(log1p_steps, 1)
                    if n == 1:
                        act.wait_ge(log1p_steps, 1)
                        act.activation(k_end[:, :, :], k_end[:, :, :], ACT.Exp, scale=-1.0)\
                           .then_inc(log1p_steps, 1)
                    if n == 2:
                        act.wait_ge(log1p_steps, 2)
                        act.activation(k_end[:, :, :], k_end[:, :, :], ACT.Ln, bias=1.0).then_inc(log1p_steps, 1)

                def exp_cum(self, n):
                    if n == 0:
                        act.wait_ge(cum_ready, 2)
                    act.activation(r_act[:, n * KEY // P:(n + 1) * KEY // P, :], cum[:, :, :], ACT.Exp,
                                   scale=(1.0 - 2.0 * n) / TAU).then_inc(exp_cum, 1)

                def tail_exp(self):
                    act.wait_ge(tail_ready, 1)
                    act.activation(k_end[:, :, :], k_end[:, :, :], ACT.Exp, scale=1.0 / TAU).then_inc(tail_exp, 1)

                def head_square(self, h):
                    act.wait_ge(s["half_free"], HEAD_GROUPS[h] + 1)
                    act.activation(head_sq[h % 2], head_out[h], ACT.Square).then_inc(head_squares, 1)

                def head_root(self, pair, at):
                    act.wait_ge(head_ms, pair + 1)
                    act.activation(head_norm(pair), head_norm(pair), ACT.Sqrt).then_inc(head_root, 1)

                def final(self):
                    for j in range(4):
                        at = At(first_of("store") + j)
                        act.wait_ge(turned, 4 + j + 1)
                        act.activation(y_tok[:, 0, j * GW:(j + 1) * GW], bank(at.half, 0), ACT.Copy)\
                           .then_inc(y_copied[0], 1)

            whole_program(act, split, Scalar())

        @block.vector
        def _(dve):
            wide_rstd = rstd[:, 0:T].unsqueeze(1).to_broadcast([P, GT, T])
            wide_rstd_sq = rstd_sq[:, :].unsqueeze(1).to_broadcast([P, GT, T])

            def split(g, a, b, turn, stride):
                for n in range(a, b):
                    i, more = sub_number(g, n, turn, stride)
                    dve.wait_ge(hi_ready, i + 1 + more)
                    dve.tensor_tensor(w_lo[:, i % SLOTS], raw_view(i), w_hi[:, i % SLOTS].bitcast(f32),
                                      ALU.subtract).then_inc(lo_ready, 1)

            def add_parts(at, out=None, half=None):
                dve.wait_ge(sub_done, at.subs_done())
                dve.tensor_reduce(summed[:, :, :], two_parts(at.half), AX.X, ALU.add).then_inc(s["half_free"], 1)
                dve.wait_ge(s["half_free"], at.groups_done(1))

            class Vector(Steps):
                def ingest_x(self, at, j):
                    dve.wait_ge(turned, j + 1)
                    dve.tensor_copy(xT[:, GT * j:GT * j + GT, :], x_turned(j)).then_inc(s["half_free"], 1)
                    if j == 0:
                        dve.wait_ge(vectors_turned, 1)
                        dve.tensor_copy(vec[:, 0:P], bank(1, 3)[:, 0:P]).then_inc(vectors_ready, 1)

                def add_x(self, at, tile0):
                    if at.g == first_of("gla_out"):
                        dve.wait_ge(s["silu"], at.value("silu", 0))
                    add_parts(at)
                    dve.tensor_tensor(xT[:, tile0:tile0 + GT, :], xT[:, tile0:tile0 + GT, :], summed[:, :, :],
                                      ALU.add).then_inc(s["x_added"], 1)

                def split_x(self, at, tile0, norm):
                    if norm < 4:
                        if GROUPS[at.g][0] == "ingest":
                            dve.wait_ge(vectors_ready, 1)
                            dve.wait_ge(s["half_free"], at.groups_done(1))
                        dve.wait_ge(s["xs_hi"], at.value("xs_hi", 1))
                        for t in range(tile0, tile0 + GT):
                            ins = dve.scalar_tensor_tensor(
                                out=xs[:, t, T:2 * T], in0=xT[:, t, :],
                                scalar=vec[:, GAIN[norm] + t:GAIN[norm] + t + 1],
                                in1=xs[:, t, 0:T].bitcast(f32), op0=ALU.mult, op1=ALU.subtract)
                        ins.then_inc(s["xs_ready"], 1)

                def square_x(self, at, tile0, norm):
                    dve.wait_ge(s["squares"], at.value("squares", 1))
                    out, done = (sum_group, group_summed) if tile0 else (sum_x, s["sumsq"])
                    dve.tensor_reduce(out[:, :], work[:, :, :].rearrange("p a t -> p t a"), AX.X, ALU.add)\
                       .then_inc(done, 1)
                    if tile0:
                        dve.wait_ge(group_summed, 3 * norm + tile0 // GT)
                        dve.wait_ge(s["sumsq"], at.value("sumsq", 0))
                        dve.tensor_tensor(sum_x[:, :], sum_x[:, :], sum_group[:, :], ALU.add)\
                           .then_inc(s["sumsq"], 1)

                def norm(self, n):
                    half = (first_of(("conv_in", "ffn0_in0", "gla_in", "ffn1_in0", "store")[n]) + 1) % 2
                    if n == 0:
                        dve.wait_ge(vectors_turned, 2)
                        dve.tensor_copy(vec[:, P:], bank(1, 3)[:, P:V_HEAD + DV // P]).then_inc(vectors_ready, 1)
                    if n == 2:
                        dve.memset(w_gate2[:, :], 0.0).then_inc(gate2_padded, 1)
                    dve.wait_ge(mean_done, n + 1)
                    dve.tensor_scalar(rstd[:, :], bank(half, 0)[:, 0:T + 2], EPS, None, ALU.add)\
                       .then_inc(ms_ready, 1)
                    dve.wait_ge(root_ready, n + 1)
                    dve.reciprocal(rstd[:, :], rstd[:, :]).then_inc(rstd_ready, 1)
                    dve.wait_ge(rstd_ready, n + 1)
                    if n == 0:
                        dve.tensor_tensor(rstd_sq[:, :], rstd[:, 0:T], rstd[:, 0:T], ALU.mult)\
                           .then_inc(rstd_sq_ready, 1)
                        dve.memset(conv_in[:, :, 0:2], 0.0).then_inc(conv_edge, 1)
                        dve.wait_ge(rstd_sq_ready, 1)
                        dve.wait_ge(conv_edge, 1)

                def conv_c(self, at):
                    add_parts(at)
                    dve.tensor_tensor(conv_gate[:, :, :], summed[:, :, :], wide_rstd_sq, ALU.mult)\
                       .then_inc(s["scaled"], 1)

                def conv_u(self, at):
                    add_parts(at)
                    dve.wait_ge(s["scaled"], at.value("scaled", 0))
                    dve.tensor_tensor(conv_in[:, :, 2:], summed[:, :, :], conv_gate[:, :, :], ALU.mult)\
                       .then_inc(s["scaled"], 1)

                def conv_tap(self, at, tap):
                    j = (at.g - first_of("conv_in")) // 3
                    if tap == 0:
                        dve.wait_ge(s["scaled"], at.value("scaled", 1))
                    else:
                        dve.wait_ge(s["taps"], at.value("taps", tap))
                    for t in range(GT):
                        col = V_CONV + tap * DT + GT * j + t
                        w = vec[:, col:col + 1]
                        if tap == 0:
                            ins = dve.tensor_scalar(conv_y[:, t, :], conv_in[:, t, 0:T], w, None, ALU.mult)
                        else:
                            ins = dve.scalar_tensor_tensor(out=conv_y[:, t, :], in0=conv_in[:, t, tap:tap + T],
                                                           scalar=w, in1=conv_y[:, t, :], op0=ALU.mult, op1=ALU.add)
                    ins.then_inc(s["taps"], 1)

                def split_mid(self, at, tiles):
                    dve.wait_ge(s["mid_hi"], at.value("mid_hi", 1))
                    dve.tensor_tensor(mid[:, tiles, T:2 * T], work[:, :, :], mid[:, tiles, 0:T].bitcast(f32),
                                      ALU.subtract).then_inc(s["mid_ready"], 1)

                def conv_b(self, at):
                    add_parts(at)
                    dve.tensor_tensor(summed[:, :, :], summed[:, :, :], wide_rstd, ALU.mult)\
                       .then_inc(s["scaled"], 1)
                    dve.wait_ge(s["scaled"], at.value("scaled", 1))
                    dve.wait_ge(s["taps"], at.value("taps", 0))
                    dve.tensor_tensor(work[:, :, :], summed[:, :, :], conv_y[:, :, :], ALU.mult)\
                       .then_inc(s["product"], 1)

                def normed(self, at, r=None):
                    if r:
                        dve.wait_ge(s["silu"], at.value("silu", 0))
                    add_parts(at)
                    dve.tensor_tensor(summed[:, :, :], summed[:, :, :], wide_rstd, ALU.mult)\
                       .then_inc(s["scaled"], 1)

                def up(self, at):
                    dve.wait_ge(s["silu"], at.value("silu", 0))
                    add_parts(at)
                    dve.tensor_tensor(summed[:, :, :], summed[:, :, :], wide_rstd, ALU.mult)\
                       .then_inc(s["scaled"], 1)
                    dve.wait_ge(s["scaled"], at.value("scaled", 1))
                    dve.tensor_tensor(work[:, :, :], work[:, :, :], summed[:, :, :], ALU.mult)\
                       .then_inc(s["product"], 1)

                def key(self, at, j):
                    add_parts(at)
                    dve.tensor_tensor(k_t[:, GT * j:GT * j + GT, :], summed[:, :, :], wide_rstd, ALU.mult)\
                       .then_inc(s["scaled"], 1)

                def query(self, at, j):
                    add_parts(at)
                    dve.scalar_tensor_tensor(out=q_t[:, GT * j:GT * j + GT, :], in0=summed[:, :, :],
                                             scalar=DK ** -0.5, in1=wide_rstd, op0=ALU.mult, op1=ALU.mult)\
                       .then_inc(s["scaled"], 1)

                def zed(self, at):
                    dve.memset(reset[:, :], 1.0).then_inc(reset_ready, 1)
                    dve.wait_ge(reset_ready, 1)
                    dve.memset(reset[:, 0:T:CHUNK], 0.0).then_inc(reset_ready, 1)
                    dve.wait_ge(sub_done, at.subs_done())
                    dve.tensor_reduce(summed[:, 0, :], bank(at.half, 0).rearrange("p (h t) -> p t h", h=2),
                                      AX.X, ALU.add).then_inc(s["half_free"], 1)
                    dve.wait_ge(s["half_free"], at.groups_done(1))
                    dve.tensor_tensor(zT[:, :], summed[:, 0, :], rstd[:, 0:T], ALU.mult)\
                       .then_inc(s["scaled"], 1)

                def logits(self, at):
                    dve.wait_ge(logits_done, 1)
                    for t in range(KEY // P):
                        ins = dve.tensor_scalar(cum[:, t, :], packed(at.half, 8)[:, t, :],
                                                vec[:, V_BIAS + t:V_BIAS + t + 1], None, ALU.add)
                    ins.then_inc(s["half_free"], 1)

                def log_decay(self):
                    dve.wait_ge(log1p_steps, 3)
                    dve.scalar_tensor_tensor(out=k_end[:, :, :], in0=cum[:, :, :], scalar=0.0, in1=k_end[:, :, :],
                                             op0=ALU.min, op1=ALU.subtract).then_inc(log_decay_ready, 1)

                def running_sum(self, tiles):
                    dve.wait_ge(log_decay_ready, 1)
                    dve.wait_ge(reset_ready, 2)
                    for t in tiles:
                        ins = dve.tensor_tensor_scan(cum[:, t, :], reset[:, :], k_end[:, t, :], 0.0,
                                                     ALU.mult, ALU.add)
                    ins.then_inc(cum_ready, 1)

                def tail(self):
                    chunks = cum[:, :, :].rearrange("p a (n c) -> p (a n) c", c=CHUNK)
                    dve.wait_ge(cum_ready, 2)
                    dve.tensor_tensor(k_end[:, :, :].rearrange("p a (n c) -> p (a n) c", c=CHUNK),
                                      chunks[:, :, CHUNK - 1:CHUNK].to_broadcast([P, KEY // P * NCHUNK, CHUNK]),
                                      chunks, ALU.subtract).then_inc(tail_ready, 1)
                    dve.wait_ge(exp_cum, 1)
                    dve.tensor_copy(decay[:, :, :], r_act[:, 0:KEY // P, CHUNK - 1::CHUNK]).then_inc(decay_ready, 1)

                def keys_end(self):
                    dve.wait_ge(tail_exp, 1)
                    dve.tensor_tensor(k_end[:, :, :], k_end[:, :, :], k_t[:, :, :], ALU.mult).then_inc(keys_ready, 1)

                def keys_near(self):
                    dve.wait_ge(exp_cum, 2)
                    dve.tensor_tensor(k_t[:, :, :], k_t[:, :, :], r_act[:, KEY // P:, :], ALU.mult)\
                       .then_inc(keys_ready, 1)

                def queries_near(self):
                    dve.tensor_tensor(q_t[:, :, :], q_t[:, :, :], r_act[:, 0:KEY // P, :], ALU.mult)\
                       .then_inc(q_ready, 1)

                def queries_far(self):
                    def over(n):
                        return decay[:, :, n:n + 1].to_broadcast([P, KEY // P, CHUNK])

                    dve.wait_ge(q_ready, 1)
                    dve.wait_ge(decay_ready, 1)
                    dve.tensor_tensor(q_far[:, :, 0, :], q_t[:, :, 2 * CHUNK:3 * CHUNK], over(1), ALU.mult)\
                       .then_inc(q_far_steps, 1)
                    dve.tensor_tensor(q_far[:, :, 2, :], q_t[:, :, 3 * CHUNK:], over(2), ALU.mult)\
                       .then_inc(q_far_steps, 1)
                    dve.wait_ge(q_far_steps, 2)
                    dve.tensor_tensor(q_far[:, :, 1, :], q_far[:, :, 2, :], over(1), ALU.mult)\
                       .then_inc(q_far_steps, 1)

                def value(self, at, j):
                    dve.wait_ge(sub_done, at.subs_done())
                    for m in range(2):
                        ins = dve.tensor_scalar(v_tok[:, m, j * GW:(j + 1) * GW], bank(at.half, m),
                                                rstd[:, T + m:T + m + 1], None, ALU.mult)
                    ins.then_inc(s["half_free"], 1)

                def scores(self, at):
                    dve.wait_ge(scores_done, 1)
                    banks = ps[:, 4 * at.half:4 * at.half + 4, :]
                    for rows, cols in ((slice(0, CHUNK), slice(0, T)), (slice(CHUNK, P), slice(CHUNK, T)),
                                       (slice(0, CHUNK), slice(T, 3 * P)),
                                       (slice(CHUNK, P), slice(T + CHUNK, 3 * P))):
                        ins = dve.tensor_copy(att[rows, :, cols], banks[rows, :, cols])
                    ins.then_inc(s["half_free"], 1)

                def head_copy(self, at, h):
                    dve.wait_ge(head_done, h + 1)
                    dve.tensor_copy(head_out[h], packed(at.half, GT)).then_inc(s["half_free"], 1)

                def head_sumsq(self, h):
                    dve.wait_ge(head_squares, h + 1)
                    dve.tensor_reduce(q_t[:, h, :], head_sq[h % 2].rearrange("p a t -> p t a"), AX.X, ALU.add)\
                       .then_inc(head_sumsq, 1)

                def head_root(self, pair, at):
                    dve.wait_ge(head_mean, 2 * pair + 2)
                    dve.tensor_scalar(head_norm(pair), ps[:, 4 * at.half + 2:4 * at.half + 4, 0:T], EPS, None,
                                      ALU.add).then_inc(head_ms, 1)

                def head_rstd(self, pair):
                    dve.wait_ge(head_root, pair + 1)
                    dve.reciprocal(head_norm(pair), head_norm(pair)).then_inc(head_rstd, 1)

                def head_scaled(self, h):
                    dve.wait_ge(head_rstd, h // 2 + 1)
                    if h == 0:
                        dve.wait_ge(head_sumsq, HEADS)
                    else:
                        dve.wait_ge(s["mid_ready"], before("mid_ready", HEAD_GROUPS[h]))
                    for e in range(GT):
                        ins = dve.scalar_tensor_tensor(out=work[:, e, :], in0=head_out[h][:, e, :],
                                                       scalar=vec[:, V_HEAD + e:V_HEAD + e + 1],
                                                       in1=q_t[:, HEADS + h, :], op0=ALU.mult, op1=ALU.mult)
                    ins.then_inc(head_scaled, 1)

                def head_product(self, at, h):
                    dve.wait_ge(head_scaled, h + 1)
                    dve.wait_ge(s["silu"], before("silu", R_GROUPS[h]) + 1)
                    dve.tensor_tensor(work[:, :, :], work[:, :, :], r_act[:, GT * h:GT * h + GT, :],
                                      ALU.mult).then_inc(s["product"], 1)

                def final(self):
                    for t in range(DT):
                        ins = dve.scalar_tensor_tensor(out=y_norm[:, t, :], in0=xT[:, t, :],
                                                       scalar=vec[:, V_FINAL + t:V_FINAL + t + 1],
                                                       in1=rstd[:, 0:T], op0=ALU.mult, op1=ALU.mult)
                        if t % GT == GT - 1:
                            ins.then_inc(y_ready, 1)
                    for j in range(4):
                        at = At(first_of("store") + j)
                        dve.wait_ge(turned, 4 + j + 1)
                        dve.tensor_copy(y_tok[:, 1, j * GW:(j + 1) * GW], bank(at.half, 1))\
                           .then_inc(y_copied[1], 1)

            whole_program(dve, split, Vector())

        @block.tensor
        def _(pe):
            def half_is_free(g, more=0):
                if g > first_of("conv_in"):
                    pe.wait_ge(s["half_free"], g - 1 + more)

            def project(g, operand, ready=None, turn=0, stride=0, before_sub=None, by_token=False):
                subs = GROUPS[g][1]
                half_is_free(g, turn * stride if stride else 0)
                for n in range(subs):
                    if before_sub and n in before_sub:
                        before_sub[n]()
                    i, more = sub_number(g, n, turn, stride)
                    if ready and n % 2 == 0:
                        pe.wait_ge(ready[0], ready[1] + n // 2 + 1)
                    pe.wait_ge(lo_ready, i + 1 + more)
                    for kk in range(SUB_K):
                        k = n * SUB_K + kk
                        start, stop = k == 0, k == subs * SUB_K - 1
                        hi, lo = w_hi[:, i % SLOTS, kk, :], w_lo[:, i % SLOTS, kk, :]
                        if by_token:
                            for m in range(2):
                                x_hi = operand[:, k, m * P:(m + 1) * P]
                                x_lo = operand[:, k, T + m * P:T + (m + 1) * P]
                                pe.matmul(bank(g % 2, m), x_hi, lo, start=start, stop=False)
                                pe.matmul(bank(g % 2, m), x_lo, hi, start=False, stop=False)
                                mm = pe.matmul(bank(g % 2, m), x_hi, hi, start=False, stop=stop)
                        else:
                            for o in range(GT):
                                cols = slice(o * P, (o + 1) * P)
                                pe.matmul(bank(g % 2, o), hi[:, cols], operand[:, k, :], start=start, stop=False)
                                mm = pe.matmul(bank(g % 2, o)[:, T:2 * T], lo[:, cols], operand[:, k, 0:T],
                                               start=False, stop=stop)
                    mm.then_inc(sub_done, 1)

            def mean_square(n, half, gap=None):
                pe.wait_ge(s["sumsq"], 4 * (n + 1))
                pe.matmul(bank(half, 0)[:, 0:T], mean_x[:, :], sum_x[:, :], start=True, stop=True)
                for m in range(2):
                    mm = pe.matmul(bank(half, 0)[:, T + m:T + m + 1], sum_x[:, m * P:(m + 1) * P], mean_x[:, 0:1],
                                   start=True, stop=True)
                mm.then_inc(mean_done, 1)

            def first_group(g, norm, also=None, mean_sub=MEAN_SUB):
                project(g, xs, ready=(s["xs_ready"], 4 * norm),
                        before_sub={**(also or {}), mean_sub: lambda: mean_square(norm, (g + 1) % 2)})
                pe.wait_ge(ms_ready, norm + 1)

            def turn_x(j):
                if j >= 2:
                    pe.wait_ge(s["half_free"], j - 1)
                pe.wait_ge(x_loaded[j], 16)
                for t in range(GT):
                    for m in range(2):
                        mm = pe.transpose(x_turned(j)[:, t, m * P:(m + 1) * P],
                                          x_tok[:, m, (GT * j + t) * P:(GT * j + t + 1) * P], ident[:, :])
                mm.then_inc(turned, 1)

            def turn_rows_b():
                rows = KEY // P + DV // P
                pe.wait_ge(rows_b_loaded, 2 * 16)
                pe.wait_ge(s["half_free"], 4)
                pe.transpose(bank(1, 3)[:, P:P + rows], rows_b[:, :], ident[0:rows, 0:rows])\
                  .then_inc(vectors_turned, 1)

            pe.wait_ge(consts_ready, 4)
            turn_x(0)
            pe.wait_ge(rows_a_loaded, 4 * 16)
            pe.transpose(bank(1, 3)[:, 0:P], rows_a[:, :], ident[:, :]).then_inc(vectors_turned, 1)
            pe.wait_ge(vectors_ready, 1)
            turn_x(1)

            g = first_of("conv_in")
            first_group(g, 0, also={2: lambda: turn_x(2), 4: lambda: turn_x(3), 6: turn_rows_b}, mean_sub=7)
            project(g + 1, xs)
            with pe.Fori(0, (count_of("conv_in") - 2) // 2) as i:
                for q in range(2):
                    project(g + 2 + q, xs, turn=i, stride=2)
            g = first_of("conv_out")
            with pe.Fori(0, 2) as i:
                for q in range(2):
                    project(g + q, mid, ready=(s["mid_ready"], before("mid_ready", g) - 4), turn=i, stride=2)

            def ffn(layer):
                for n, pairs in enumerate(PIECES):
                    g = first_of(f"ffn{layer}_in{n}")
                    done = 0
                    if n == 0:
                        first_group(g, 2 * layer + 1)
                        project(g + 1, xs)
                        done = 2
                    with pe.Fori(0, pairs - done // 2) as i:
                        for q in range(2):
                            project(g + done + q, xs, turn=i, stride=2)
                    g = first_of(f"ffn{layer}_out{n}")
                    with pe.Fori(0, 2) as i:
                        for q in range(2):
                            project(g + q, mid, ready=(s["mid_ready"], before("mid_ready", g) - pairs),
                                    turn=i, stride=2)

            ffn(0)

            g = first_of("gla_in")
            K0, Z, K1, Y, Q0, Q1, V0, V1, V2, V3, R0, S, R1, H0, H1, R2, H2, H3, R3 = \
                range(first_of("gla_in"), first_of("gla_out"))
            first_group(K0, 2)
            half_is_free(Z)
            for n in range(2):
                i = sub_before(Z) + n
                pe.wait_ge(lo_ready, i + 1)
                hi = w_hi[:, i % SLOTS].rearrange("p a n -> p (a n)").rearrange("p (k n) -> p k n", n=P)
                lo = w_lo[:, i % SLOTS].rearrange("p a n -> p (a n)").rearrange("p (k n) -> p k n", n=P)
                for kk in range(DT // 2):
                    k = n * DT // 2 + kk
                    pe.matmul(bank(Z % 2, 0), hi[:, kk, :], xs[:, k, :], start=k == 0, stop=False)
                    mm = pe.matmul(bank(Z % 2, 0)[:, T:2 * T], lo[:, kk, :], xs[:, k, 0:T], start=False,
                                   stop=k == DT - 1)
                mm.then_inc(sub_done, 1)
            project(K1, xs)
            half_is_free(Y)
            pe.wait_ge(s["scaled"], before("scaled", Z) + 1)
            pe.wait_ge(gate2_loaded, 16)
            for t in range(KEY // P):
                mm = pe.matmul(packed(Y % 2, 8)[:, t, :], w_gate2[:, t * P:(t + 1) * P], zT[:, :],
                               start=True, stop=True)
            mm.then_inc(logits_done, 1)
            project(Q0, xs)
            project(Q1, xs)
            for j in range(4):
                project(V0 + j, xs, by_token=True)
            project(R0, xs)

            half_is_free(S)
            pe.wait_ge(keys_ready, 2)
            pe.wait_ge(q_far_steps, 3)
            for h in range(HEADS):
                for m in range(NCHUNK):
                    keys = slice(m * CHUNK, (m + 1) * CHUNK)
                    rows = slice(CHUNK * (m % 2), CHUNK * (m % 2) + CHUNK)
                    base = T - P if m >= 2 else 0
                    jobs = [(k_t, m, lambda d, m=m: q_t[:, d, m * CHUNK:(m + 1) * CHUNK], 1)]
                    if m + 1 < NCHUNK:
                        jobs.append((k_end, m + 1, lambda d, m=m: q_t[:, d, (m + 1) * CHUNK:(m + 2) * CHUNK], 1))
                    if m == 0:
                        jobs.append((k_end, 2, lambda d: q_far[:, d, 0:2, :].rearrange("p a c -> p (a c)"), 2))
                    if m == 1:
                        jobs.append((k_end, 3, lambda d: q_far[:, d, 2, :], 1))
                    for src, c, query, width in jobs:
                        dst = bank(S % 2, h)[rows, base + c * CHUNK:base + (c + width) * CHUNK]
                        for half in range(2):
                            d = 2 * h + half
                            mm = pe.matmul(dst, src[:, d, keys], query(d), start=half == 0, stop=half == 1)
            mm.then_inc(scores_done, 1)

            def head(g, h):
                half_is_free(g)
                if h == 0:
                    pe.wait_ge(att_masked, 2)
                for e in range(GT):
                    cols = slice(h * DV + e * P, h * DV + (e + 1) * P)
                    dst = packed(g % 2, GT)[:, e, :]
                    pe.matmul(dst, v_tok[:, 0, cols], att[:, h, 0:T], start=True, stop=False)
                    mm = pe.matmul(dst[:, P:T], v_tok[:, 1, cols], att[:, h, T:3 * P], start=False, stop=True)
                mm.then_inc(head_done, 1)

            def head_mean_squares(g, pair):
                pe.wait_ge(head_sumsq, 2 * pair + 2)
                for h in (2 * pair, 2 * pair + 1):
                    pe.matmul(bank(g % 2, 2 + h % 2)[:, 0:T], mean_head[:, :], q_t[:, h, :], start=True, stop=True)\
                      .then_inc(head_mean, 1)

            project(R1, xs)
            head(H0, 0)
            head(H1, 1)
            project(R2, xs, before_sub={6: lambda: head_mean_squares(H1, 0)})
            head(H2, 2)
            head(H3, 3)
            pe.wait_ge(head_ms, 1)
            project(R3, xs, before_sub={6: lambda: head_mean_squares(H3, 1)})
            pe.wait_ge(head_ms, 2)
            g = first_of("gla_out")
            with pe.Fori(0, 2) as i:
                for q in range(2):
                    project(g + q, mid, ready=(s["mid_ready"], before("mid_ready", g) - 4), turn=i, stride=2)
            ffn(1)

            g = first_of("store")
            mean_square(4, (g + 1) % 2)
            for j in range(4):
                half = (g + j) % 2
                pe.wait_ge(y_ready, j + 1)
                if j >= 2:
                    pe.wait_ge(y_copied[0], j - 1)
                    pe.wait_ge(y_copied[1], j - 1)
                for m in range(2):
                    for t in range(GT):
                        mm = pe.transpose(bank(half, m)[:, t * P:(t + 1) * P],
                                          y_norm[:, GT * j + t, m * P:(m + 1) * P], ident[:, :])
                mm.then_inc(turned, 1)


def kernel(**inputs):
    import numpy as np
    import concourse.bacc as bacc
    from concourse.bass_utils import run_bass_kernel_spmd

    shapes = {
        "x": (T, D), "norm_mix": (2, D), "norm_ffn": (2, D), "norm_final": (D,), "conv_w_in": (D, 3 * D),
        "conv_w": (3, D), "conv_w_out": (D, D), "gla_w_in": (D, GLA_COLS), "gla_w_gate2": (RANK, KEY),
        "gla_b_gate": (KEY,), "gla_norm": (DV,), "gla_w_out": (D, D), "ffn_w_in": (2, D, 2 * F),
        "ffn_w_out": (2, F, D),
    }
    nc = bacc.Bacc("TRN2", target_bir_lowering=False, num_devices=1)
    arrays, args = {}, []
    for name, shape in shapes.items():
        a = np.ascontiguousarray(inputs[name]).reshape(shape)
        arrays[f"in_{name}"] = a
        args.append(nc.dram_tensor(f"in_{name}", shape, mybir.dt.from_np(a.dtype), kind="ExternalInput").ap())
    args.append(nc.dram_tensor("trunk_out", (T, D), mybir.dt.float32, kind="ExternalOutput").ap())
    trunk(nc, *args)
    r = run_bass_kernel_spmd(nc, [arrays], core_ids=[0])
    return r.results[0]["trunk_out"].reshape(1, T, D)
```

```python
import concourse.bass as bass
from concourse import mybir
from contextlib import ExitStack


P = 128
T = 256
D = 2048
DT = D // P
GW = 512
GT = GW // P
F = 5632
PAIRS = F // GW
PIECES = (4, 4, 3)
HEADS, DK, DV, CHUNK, RANK = 4, 256, 512, 64, 16
KEY = HEADS * DK
NCHUNK = T // CHUNK
GLA_COLS = 2 * KEY + 2 * D + RANK
EPS = 1e-6
TAU = 16.0
SLOTS = 4
SUB_K = 2
MEAN_SUB = 6
HEAD_MEAN_SUB = 5

V_MIX, V_FFN, V_FINAL, V_CONV, V_BIAS, V_HEAD = 0, 2 * DT, 4 * DT, 5 * DT, 8 * DT, 8 * DT + KEY // P

ADDS = {
    "ingest": dict(half_free=1, xs_hi=1, squares=1, xs_ready=1, sumsq=1),
    "partial": dict(half_free=1, x_added=1),
    "finish": dict(half_free=1, x_added=1, xs_hi=1, squares=1, xs_ready=1, sumsq=1),
    "conv_c": dict(half_free=1, scaled=1),
    "conv_u": dict(half_free=1, scaled=1, taps=3),
    "conv_b": dict(half_free=1, scaled=1, product=1, mid_hi=1, mid_ready=1),
    "gate": dict(half_free=1, scaled=1, silu=1),
    "up": dict(half_free=1, scaled=1, product=1, mid_hi=1, mid_ready=1),
    "key": dict(half_free=1, scaled=1),
    "query": dict(half_free=1, scaled=1),
    "zed": dict(half_free=1, scaled=1),
    "logits": dict(half_free=1),
    "value": dict(half_free=1),
    "scores": dict(half_free=1),
    "head": dict(half_free=1, product=1, mid_hi=1, mid_ready=1),
}
NO_WEIGHTS = ("ingest", "logits", "scores", "head")


def schedule():
    groups = [("ingest", 0, "ingest")] * 4
    groups += [("conv_c", 8, "conv_in"), ("conv_u", 8, "conv_in"), ("conv_b", 8, "conv_in")] * 4
    groups += [("finish", 8, "conv_out")] * 4

    def ffn(layer):
        out = []
        for n, pairs in enumerate(PIECES):
            out += [("gate", 8, f"ffn{layer}_in{n}"), ("up", 8, f"ffn{layer}_in{n}")] * pairs
            kind = "finish" if n == len(PIECES) - 1 else "partial"
            out += [(kind, 2 * pairs, f"ffn{layer}_out{n}")] * 4
        return out

    groups += ffn(0)
    for kind in ("key", "zed", "key", "logits", "query", "query", "value", "value", "value", "value",
                 "gate", "scores", "gate", "head", "head", "gate", "head", "head", "gate"):
        groups.append((kind, 0 if kind in NO_WEIGHTS else 2 if kind == "zed" else 8, "gla_in"))
    groups += [("finish", 8, "gla_out")] * 4
    groups += ffn(1)
    return groups


GROUPS = schedule()


def first_of(phase):
    return [p for _, _, p in GROUPS].index(phase)


def count_of(phase):
    return sum(p == phase for _, _, p in GROUPS)


def sub_before(g):
    return sum(s for _, s, _ in GROUPS[:g])


def before(name, g):
    return sum(ADDS[k].get(name, 0) for k, _, _ in GROUPS[:g])


class At:

    def __init__(self, g, turn=0, cycle=0):
        self.g, self.turn, self.cycle = g, turn, cycle
        self.half = g % 2

    def value(self, name, more):
        step = before(name, self.g + self.cycle) - before(name, self.g)
        return before(name, self.g) + more + (self.turn * step if self.cycle else 0)

    def subs_done(self):
        step = sub_before(self.g + self.cycle) - sub_before(self.g)
        return sub_before(self.g + 1) + (self.turn * step if self.cycle else 0)

    def groups_done(self, more):
        return self.g + more + (self.turn * self.cycle if self.cycle else 0)


def trunk(nc, x, norm_mix, norm_ffn, norm_final, conv_w_in, conv_w, conv_w_out, gla_w_in, gla_w_gate2,
          gla_b_gate, gla_norm, gla_w_out, ffn_w_in, ffn_w_out, out):
    f32, f32r = mybir.dt.float32, mybir.dt.float32r
    ACT, ALU, AX = mybir.ActivationFunctionType, mybir.AluOpType, mybir.AxisListType
    ctx = ExitStack()
    with ctx:
        def sb(name, shape, dt=f32, where=None):
            return (where or ctx).enter_context(nc.sbuf_tensor(name, shape, dt))

        def sem(name):
            return ctx.enter_context(nc.semaphore(name))

        xT = sb("xT", [P, DT, T])
        xs = sb("xs", [P, DT, 2 * T], f32r)
        raw = sb("raw", [P, SLOTS, 4, GW])
        w_hi = sb("w_hi", [P, SLOTS, SUB_K, GW], f32r)
        w_lo = sb("w_lo", [P, SLOTS, SUB_K, GW], f32r)
        summed = sb("summed", [P, GT, T])
        work = sb("work", [P, GT, T])
        sum_x = sb("sum_x", [P, T])
        sum_group = sb("sum_group", [P, T])
        rstd = sb("rstd", [P, T + 2])
        rstd_sq = sb("rstd_sq", [P, T])
        vec = sb("vec", [P, V_HEAD + DV // P])
        ident = sb("ident", [P, P])
        decay = sb("decay", [P, KEY // P, NCHUNK])
        mean_x = sb("mean_x", [P, P])
        mean_head = sb("mean_head", [P, P])

        with ExitStack() as use:
            q_far = sb("q_far", [P, KEY // P, 3, CHUNK], where=use)
            w_gate2 = sb("w_gate2", [P, KEY], where=use)
            zT = sb("zT", [P, T], where=use)
            reset = sb("reset", [P, T], where=use)
            head_sq_third = sb("head_sq_third", [P, GT, T], where=use)
            r_act = sb("r_act", [P, DT, T], where=use)
        mid = sb("mid", [P, DT, 2 * T], f32r)

        with ExitStack() as use:
            x_tok = sb("x_tok", [P, 2, D], where=use)
            rows_a = sb("rows_a", [P, P], where=use)
            rows_b = sb("rows_b", [KEY // P + DV // P, P], where=use)
        with ExitStack() as use:
            conv_gate = sb("conv_gate", [P, GT, T], where=use)
            conv_in = sb("conv_in", [P, GT, T + 2], where=use)
            conv_y = sb("conv_y", [P, GT, T], where=use)
        with ExitStack() as use:
            y_gain = sb("y_gain", [P, DT, T], where=use)
            y_tok = sb("y_tok", [P, 2, D], where=use)
        cum = sb("cum", [P, KEY // P, T])
        q_t = sb("q_t", [P, KEY // P, T])
        k_t = sb("k_t", [P, KEY // P, T])
        k_end = sb("k_end", [P, KEY // P, T])
        v_tok = sb("v_tok", [P, 2, D])
        head_out = [buf[:, GT * a:GT * a + GT, :] for buf in (k_t, k_end) for a in range(2)]
        att = cum[:, :, :].rearrange("p a t -> p (a t)")[:, 0:HEADS * 3 * P].rearrange("p (h c) -> p h c", h=HEADS)

        ps = ctx.enter_context(nc.psum_tensor("ps", [P, 8, GW], f32))

        raw_loaded = [sem(f"raw_loaded{i}") for i in range(SLOTS)]
        hi_ready = sem("hi_ready")
        lo_ready = sem("lo_ready")
        sub_done = sem("sub_done")
        x_loaded = [sem(f"x_loaded{j}") for j in range(4)]
        rows_a_loaded = sem("rows_a_loaded")
        rows_b_loaded = sem("rows_b_loaded")
        gate2_loaded = sem("gate2_loaded")
        consts_ready = sem("consts_ready")
        vectors_turned = sem("vectors_turned")
        vectors_ready = sem("vectors_ready")
        turned = sem("turned")
        s = {n: sem(n) for n in ("half_free", "x_added", "xs_hi", "squares", "xs_ready", "sumsq", "scaled",
                                 "taps", "product", "mid_hi", "mid_ready", "silu")}
        group_summed = sem("group_summed")
        mean_done = sem("mean_done")
        ms_ready = sem("ms_ready")
        root_ready = sem("root_ready")
        rstd_ready = sem("rstd_ready")
        rstd_sq_ready = sem("rstd_sq_ready")
        conv_edge = sem("conv_edge")
        gate2_padded = sem("gate2_padded")
        reset_ready = sem("reset_ready")
        logits_done = sem("logits_done")
        log1p_steps = sem("log1p_steps")
        log_decay_ready = sem("log_decay_ready")
        cum_ready = sem("cum_ready")
        exp_cum = sem("exp_cum")
        tail_ready = sem("tail_ready")
        tail_exp = sem("tail_exp")
        decay_ready = sem("decay_ready")
        keys_ready = sem("keys_ready")
        q_ready = sem("q_ready")
        q_far_steps = sem("q_far_steps")
        scores_done = sem("scores_done")
        att_masked = sem("att_masked")
        head_done = sem("head_done")
        head_squares = sem("head_squares")
        head_sumsq = sem("head_sumsq")
        head_mean = sem("head_mean")
        head_ms = sem("head_ms")
        head_root = sem("head_root")
        head_rstd = sem("head_rstd")
        head_gained = sem("head_gained")
        head_gated = sem("head_gated")
        y_gained = sem("y_gained")
        y_copied = [sem("y_copied0"), sem("y_copied1")]
        last_hi_added = sem("last_hi_added")
        last_added = sem("last_added")
        last_squares = sem("last_squares")
        y_scaled = [sem("y_scaled0"), sem("y_scaled1")]
        stored = sem("stored")

        def bank(half, b):
            return ps[:, 4 * half + b, :]

        def two_parts(half):
            return ps[:, 4 * half:4 * half + 4, :].rearrange("p b (h t) -> p b t h", h=2)

        def packed(half, tiles):
            return ps[:, 4 * half:4 * half + tiles // 2, :].rearrange("p b (a t) -> p (b a) t", a=2)

        GAIN = [V_MIX, V_FFN, V_MIX + DT, V_FFN + DT]
        R_GROUPS = [g for g, (k, _, p) in enumerate(GROUPS) if k == "gate" and p == "gla_in"]
        HEAD_GROUPS = [g for g, (k, _, _) in enumerate(GROUPS) if k == "head"]
        Y_READ = [k for k, _, _ in GROUPS].index("logits") + 1
        last_r = r_act[:, DT - GT:DT, :]
        head_sq = [work[:, :, :], last_r, head_sq_third[:, :, :], last_r]

        def x_turned(j):
            return ps[:, 4 + 2 * (j % 2):6 + 2 * (j % 2), :].rearrange("p b (a t) -> p (b a) t", a=2)

        def head_norm(pair):
            return q_t[:, HEADS + 2 * pair:HEADS + 2 * pair + 2, :]

        LAST = len(GROUPS) - 1

        y_means = ps[:, 4 * ((LAST + 1) % 2):4 * ((LAST + 1) % 2) + 2, :]

        def y_turned(j, m):
            return bank((LAST + 1) % 2, 2 * (j % 2) + m)

        FINISH_GROUPS = [g for g, (k, _, _) in enumerate(GROUPS) if k in ("ingest", "finish")]

        block = ctx.enter_context(nc.Block())

        @block.sync
        def _(sp):
            def chunk(c, src, turn=0, step=0, view=None):
                slot = c % SLOTS
                if c >= SLOTS or step:
                    sp.wait_ge(lo_ready, 2 * (c - SLOTS) + 2 + (turn * (2 * step) if step else 0))
                dst = raw[:, slot] if view is None else raw[:, slot].rearrange("p a n -> p (a n)")\
                    .rearrange("p (k n) -> p k n", n=view)
                sp.dma_start(dst, src).then_inc(raw_loaded[slot], 16)

            def matrix(w):
                return w.rearrange("(k p) n -> p k n", p=P)

            def group(c, w, k0, kn, col, turn=0, step=0):
                for n in range(kn // 4):
                    chunk(c + n, w[:, k0 + 4 * n:k0 + 4 * n + 4, bass.ds(col, GW)], turn, step)
                return c + kn // 4

            def x_columns(j):
                sp.dma_start(x_tok[:, :, j * GW:(j + 1) * GW],
                             x.rearrange("(m p) n -> p m n", p=P)[:, :, j * GW:(j + 1) * GW])\
                  .then_inc(x_loaded[j], 16)

            w = matrix(conv_w_in)
            x_columns(0)
            for row, src in ((V_MIX, norm_mix), (V_FFN, norm_ffn), (V_CONV, conv_w)):
                n = src.shape[0] * DT
                sp.dma_start(rows_a[row:row + n, :], src.rearrange("l (k p) -> (l k) p", p=P))\
                  .then_inc(rows_a_loaded, 16)
            sp.dma_start(rows_a[V_FINAL:V_FINAL + DT, :], norm_final.rearrange("(k p) -> k p", p=P))\
              .then_inc(rows_a_loaded, 16)
            x_columns(1)
            for j in range(4):
                chunk(j, w[:, 4 * j:4 * j + 4, D:D + GW])
                if j < 2:
                    x_columns(2 + j)
            c = 4
            for part in (2, 0):
                c = group(c, w, 0, DT, part * D)
            with sp.Fori(0, D // GW - 1) as i:
                for n, part in enumerate((1, 2, 0)):
                    group(c + 4 * n, w, 0, DT, i * GW + (part * D + GW), i, 12)
            c += 12 * (D // GW - 1)
            with sp.Fori(0, D // GW) as i:
                group(c, matrix(conv_w_out), 0, DT, i * GW, i, 4)
            c += 4 * (D // GW)

            def ffn(c, layer):
                w_in, w_out = matrix(ffn_w_in[layer]), matrix(ffn_w_out[layer])
                k0 = 0
                for pairs in PIECES:
                    with sp.Fori(0, pairs) as i:
                        group(c, w_in, 0, DT, i * GW + k0 * P, i, 8)
                        group(c + 4, w_in, 0, DT, i * GW + (F + k0 * P), i, 8)
                    c += 8 * pairs
                    if pairs == SLOTS:
                        with sp.Fori(0, D // GW) as i:
                            group(c, w_out, k0, 4 * pairs, i * GW, i, pairs)
                        c += pairs * (D // GW)
                    else:
                        for n in range(D // GW):
                            c = group(c, w_out, k0, 4 * pairs, n * GW)
                    k0 += 4 * pairs
                return c

            c = ffn(c, 0)
            w = matrix(gla_w_in)
            c = group(c, w, 0, DT, KEY)
            chunk(c, w[:, :, GLA_COLS - P:GLA_COLS], view=P)
            c = group(c + 1, w, 0, DT, KEY + GW)
            for col in (0, GW):
                c = group(c, w, 0, DT, col)
            with sp.Fori(0, 2 * D // GW) as i:
                group(c, w, 0, DT, i * GW + 2 * KEY, i, 4)
            c += 4 * (2 * D // GW)
            with sp.Fori(0, D // GW) as i:
                group(c, matrix(gla_w_out), 0, DT, i * GW, i, 4)
            c += 4 * (D // GW)
            ffn(c, 1)
            for j in range(4):
                sp.wait_ge(y_scaled[0], j + 1)
                sp.wait_ge(y_scaled[1], j + 1)
                sp.dma_start(out.rearrange("(m p) n -> p m n", p=P)[:, :, j * GW:(j + 1) * GW],
                             y_tok[:, :, j * GW:(j + 1) * GW]).then_inc(stored, 16)
            sp.wait_ge(stored, 4 * 16)

        @block.gpsimd
        def _(pool):
            pool.memset(ident[:, :], 0.0).then_inc(consts_ready, 1)
            pool.memset(mean_x[:, :], 1.0 / D).then_inc(consts_ready, 1)
            pool.memset(mean_head[:, :], 1.0 / DV).then_inc(consts_ready, 1)
            pool.wait_ge(consts_ready, 3)
            pool.affine_select(out=ident[:, :], in_=ident[:, :], compare_op=ALU.not_equal, fill=1.0, base=0,
                               pattern=[[-1, P]], channel_multiplier=1).then_inc(consts_ready, 1)
            pool.wait_ge(s["half_free"], first_of("gla_in") + 12)
            pool.affine_select(out=att[:, :, 0:T], in_=att[:, :, 0:T], compare_op=ALU.is_ge, fill=0.0, base=0,
                               pattern=[[0, HEADS], [1, T]], channel_multiplier=-1).then_inc(att_masked, 1)
            pool.affine_select(out=att[:, :, T:3 * P], in_=att[:, :, T:3 * P], compare_op=ALU.is_ge, fill=0.0,
                               base=0, pattern=[[0, HEADS], [1, P]], channel_multiplier=-1).then_inc(att_masked, 1)

        def one(split, g, slots, turn=0, stride=0):
            subs = GROUPS[g][1]
            early = min(SLOTS - 1, subs) if -1 in slots else min(SLOTS, subs)
            split(g, 0, early, turn, stride)
            for step in slots.get(-1, ()):
                step()
            split(g, early, min(SLOTS, subs), turn, stride)
            for n in range(5):
                for step in slots.get(n, ()):
                    step()
                if SLOTS + n < subs:
                    split(g, SLOTS + n, SLOTS + n + 1, turn, stride)

        def run(eng, split, pending, g0, n, readouts, looped, after_first=None, first_done=False):
            cycle = len(readouts)
            turns = n // cycle
            if not first_done:
                one(split, g0, pending)
            if after_first:
                after_first()
            if looped:
                with eng.Fori(0, turns - 1) as i:
                    for q in range(1, cycle + 1):
                        one(split, g0 + q, readouts[q - 1](At(g0 + q - 1, i, cycle)), i, cycle)
            else:
                for q in range(1, (turns - 1) * cycle + 1):
                    one(split, g0 + q, readouts[(q - 1) % cycle](At(g0 + q - 1)))
            last = g0 + (turns - 1) * cycle
            for q in range(1, cycle):
                one(split, last + q, readouts[q - 1](At(last + q - 1)))
            return readouts[cycle - 1](At(last + cycle - 1))

        def sub_number(g, n, turn, stride):
            return sub_before(g) + n, turn * (sub_before(g + stride) - sub_before(g)) if stride else 0

        def raw_view(i):
            return raw[:, i // 2 % SLOTS, SUB_K * (i % 2):SUB_K * (i % 2) + SUB_K, :]

        def mid_tiles(at, phase_first, per):
            t0 = (at.g - phase_first) // per * GT
            if at.cycle:
                return bass.ds(at.turn * (at.cycle // per * GT) + t0, GT)
            return slice(t0, t0 + GT)

        class Steps:

            def ingest_x(self, at, j): pass
            def add_x(self, at, tile0): pass
            def split_x(self, at, tile0, norm): pass
            def square_x(self, at, tile0, norm): pass
            def more_vectors(self): pass
            def norm(self, n): pass
            def add_conv_c(self, at): pass
            def scale_conv_c(self, at): pass
            def conv_u(self, at): pass
            def conv_tap(self, at, tap): pass
            def conv_b(self, at): pass
            def split_mid(self, at, tiles): pass
            def normed(self, at, r=None): pass
            def silu(self, at, r=None): pass
            def up(self, at): pass
            def key(self, at, j): pass
            def zed(self, at): pass
            def load_gate2(self): pass
            def logits(self, at): pass
            def log1p(self, n): pass
            def query(self, at, j): pass
            def log_decay(self): pass
            def running_sum(self, tiles): pass
            def exp_cum(self, n): pass
            def tail(self): pass
            def tail_exp(self): pass
            def value(self, at, j): pass
            def keys_end(self): pass
            def keys_near(self): pass
            def queries_near(self): pass
            def queries_far(self): pass
            def scores(self, at): pass
            def head_copy(self, h): pass
            def head_gain(self, h): pass
            def head_gated(self, h): pass
            def head_square(self, h): pass
            def head_sumsq(self, h): pass
            def head_root(self, pair, at): pass
            def head_rstd(self, h): pass
            def head_scaled(self, h): pass
            def copy_y(self, j): pass
            def last_group(self): pass
            def last_norm(self): pass
            def scale_y(self): pass

        def whole_program(eng, split, e):
            def finish(norm):
                def readout(at):
                    tile0 = GT * (FINISH_GROUPS.index(at.g) % 4)
                    return {0: [lambda: e.add_x(at, tile0)], 2: [lambda: e.split_x(at, tile0, norm)],
                            3: [lambda: e.square_x(at, tile0, norm)]}
                return readout

            def partial(at):
                return {0: [lambda: e.add_x(at, GT * (at.g - first_of(GROUPS[at.g][2])))]}

            def conv_c(at):
                if at.g == first_of("conv_in"):
                    return {0: [lambda: e.square_x(At(3), 3 * GT, 0), lambda: e.add_conv_c(at)],
                            2: [lambda: e.norm(0), lambda: e.scale_conv_c(at)]}
                return {0: [lambda: e.add_conv_c(at), lambda: e.scale_conv_c(at)]}

            def conv_u(at):
                return {0: [lambda: e.conv_u(at)]} | {1 + k: [lambda k=k: e.conv_tap(at, k)] for k in range(3)}

            def conv_b(at):
                return {0: [lambda: e.conv_b(at)],
                        2: [lambda: e.split_mid(at, mid_tiles(at, first_of("conv_in"), 3))]}

            def gate(at):
                return {0: [lambda: e.normed(at)], 2: [lambda: e.silu(at)]}

            def up_of(first):
                return lambda at: {0: [lambda: e.up(at)], 2: [lambda: e.split_mid(at, mid_tiles(at, first, 2))]}

            g = first_of("conv_in")
            e.ingest_x(At(0), 0)
            for j in range(4):
                e.split_x(At(j), GT * j, 0)
                split(g, 2 * j, 2 * j + 1, 0, 0)
                if 0 < j < 3:
                    e.square_x(At(j - 1), GT * (j - 1), 0)
                if j < 3:
                    e.ingest_x(At(j + 1), j + 1)
                split(g, 2 * j + 1, 2 * j + 2, 0, 0)
            e.square_x(At(2), 2 * GT, 0)
            e.more_vectors()
            pend = run(eng, split, None, g, 12, [conv_c, conv_u, conv_b], False, first_done=True)
            pend = run(eng, split, pend, first_of("conv_out"), 4, [finish(1)], False)

            def ffn(layer, pend):
                for n, pairs in enumerate(PIECES):
                    g = first_of(f"ffn{layer}_in{n}")
                    pend = run(eng, split, pend, g, 2 * pairs, [gate, up_of(g)], True,
                               (lambda: e.norm(2 * layer + 1)) if n == 0 else None)
                    last = n == len(PIECES) - 1
                    g = first_of(f"ffn{layer}_out{n}")
                    if g + 3 < LAST:
                        pend = run(eng, split, pend, g, 4, [finish(2 * layer + 2) if last else partial], False)
                    else:
                        pend = run(eng, split, pend, g, 3, [finish(4)], False)
                        one(split, LAST, {0: pend[0], 1: [lambda: e.copy_y(0)],
                                          2: pend[2] + [lambda: e.copy_y(1)] + pend[3] + [lambda: e.copy_y(2)]})
                return pend

            pend = ffn(0, pend)
            K0, Z, K1, Y, Q0, Q1, V0, V1, V2, V3, R0, S, R1, H0, H1, R2, H2, H3, R3 = \
                range(first_of("gla_in"), first_of("gla_out"))

            def weights_of(group, slots):
                one(split, group, slots)

            def each(*steps):
                return [(lambda f=f, a=a: f(*a)) for f, *a in steps]

            weights_of(K0, pend)
            e.norm(2)
            weights_of(Z, {0: each((e.key, At(K0), 0), (e.load_gate2,))})
            weights_of(K1, {0: each((e.zed, At(Z)))})
            weights_of(Q0, {-1: each((e.key, At(K1), 1)), 2: each((e.logits, At(Y)), (e.log1p, 0)),
                            3: each((e.log1p, 1))})
            weights_of(Q1, {0: each((e.query, At(Q0), 0), (e.log1p, 2)), 1: each((e.log_decay,)),
                            2: each((e.running_sum, range(0, 4))), 3: each((e.running_sum, range(4, 8))),
                            4: each((e.exp_cum, 0))})
            weights_of(V0, {0: each((e.query, At(Q1), 1)), 1: each((e.tail,), (e.exp_cum, 1)),
                            3: each((e.tail_exp,))})
            weights_of(V1, {0: each((e.value, At(V0), 0)), 1: each((e.keys_end,)), 3: each((e.keys_near,))})
            weights_of(V2, {0: each((e.value, At(V1), 1)), 1: each((e.queries_near,)), 3: each((e.queries_far,))})
            weights_of(V3, {0: each((e.value, At(V2), 2))})
            weights_of(R0, {0: each((e.value, At(V3), 3))})
            weights_of(R1, {0: each((e.normed, At(R0), 0), (e.scores, At(S))), 2: each((e.silu, At(R0), 0)), 3: each((e.head_gain, 0),)})
            weights_of(R2, {-1: each((e.normed, At(R1), 1)), 0: each((e.head_copy, 0), (e.head_copy, 1)),
                            1: each((e.head_square, 0), (e.head_square, 1), (e.silu, At(R1), 1)),
                            2: each((e.head_gain, 1), (e.head_sumsq, 0), (e.head_sumsq, 1)),
                            3: each((e.head_gated, 0),),
                            4: each((e.head_gated, 1), (e.head_root, 0, At(H1)))})
            weights_of(R3, {-1: each((e.normed, At(R2), 2)),
                            0: each((e.head_copy, 2), (e.head_copy, 3), (e.head_square, 2), (e.head_square, 3),
                                    (e.head_rstd, 0), (e.head_rstd, 1)),
                            1: each((e.head_sumsq, 2), (e.head_sumsq, 3), (e.silu, At(R2), 2)),
                            2: each((e.head_gain, 2), (e.head_scaled, 0), (e.split_mid, At(H0), slice(0, GT))),
                            3: each((e.head_root, 1, At(H3)), (e.head_scaled, 1), (e.head_gated, 2)),
                            4: each((e.split_mid, At(H1), slice(GT, 2 * GT)), (e.head_rstd, 2))})
            pend = {-1: each((e.normed, At(R3), 3)),
                    0: each((e.silu, At(R3), 3), (e.head_scaled, 2)),
                    1: each((e.split_mid, At(H2), slice(2 * GT, 3 * GT)), (e.head_gain, 3), (e.head_rstd, 3), (e.head_gated, 3)),
                    2: each((e.head_scaled, 3),),
                    3: each((e.split_mid, At(H3), slice(3 * GT, 4 * GT)))}
            pend = run(eng, split, pend, first_of("gla_out"), 4, [finish(3)], False)
            ffn(1, pend)
            e.last_group()
            e.last_norm()
            e.scale_y()

        @block.scalar
        def _(act):
            act.wait_ge(consts_ready, 3)
            act.activation(sum_group[:, 0:P], mean_x[:, :], ACT.Copy)
            act.dma_start(rows_b[0:KEY // P, :], gla_b_gate.rearrange("(k p) -> k p", p=P))\
               .then_inc(rows_b_loaded, 16)
            act.dma_start(rows_b[KEY // P:, :], gla_norm.rearrange("(k p) -> k p", p=P)).then_inc(rows_b_loaded, 16)

            def split(g, a, b, turn, stride):
                for n in range(a, b):
                    i, more = sub_number(g, n, turn, stride)
                    if i % 2 == 0:
                        act.wait_ge(raw_loaded[i // 2 % SLOTS], 16 * (i // 2 // SLOTS + 1) + more * 2)
                    if i >= SLOTS:
                        act.wait_ge(sub_done, i - SLOTS + 1 + more)
                    act.activation(w_hi[:, i % SLOTS], raw_view(i), ACT.Copy).then_inc(hi_ready, 1)

            class Scalar(Steps):
                def split_x(self, at, tile0, norm):
                    if norm == 4:
                        act.wait_ge(s["x_added"], at.value("x_added", 1))
                        self.gain_y(range(tile0, tile0 + GT))
                    else:
                        if GROUPS[at.g][0] == "finish":
                            act.wait_ge(s["x_added"], at.value("x_added", 1))
                        else:
                            if at.g == 0:
                                act.wait_ge(vectors_ready, 1)
                            act.wait_ge(s["half_free"], at.groups_done(1))
                        for t in range(tile0, tile0 + GT):
                            ins = act.activation(xs[:, t, 0:T], xT[:, t, :], ACT.Copy,
                                                 scale=vec[:, GAIN[norm] + t:GAIN[norm] + t + 1])
                        ins.then_inc(s["xs_hi"], 1)

                def square_x(self, at, tile0, norm):
                    if at.value("sumsq", 0):
                        act.wait_ge(s["sumsq"], at.value("sumsq", 0))
                    act.activation(work[:, :, :], xT[:, tile0:tile0 + GT, :], ACT.Square)\
                       .then_inc(s["squares"], 1)

                def norm(self, n):
                    act.wait_ge(ms_ready, n + 1)
                    act.activation(rstd[:, :], rstd[:, :], ACT.Sqrt).then_inc(root_ready, 1)

                def load_gate2(self):
                    act.wait_ge(gate2_padded, 1)
                    act.dma_start(w_gate2[P - RANK:, :], gla_w_gate2).then_inc(gate2_loaded, 16)

                def split_mid(self, at, tiles):
                    act.wait_ge(s["product"], at.value("product", 1))
                    act.activation(mid[:, tiles, 0:T], work[:, :, :], ACT.Copy).then_inc(s["mid_hi"], 1)

                def silu(self, at, r=None):
                    act.wait_ge(s["scaled"], at.value("scaled", 1))
                    dst = work[:, :, :] if r is None else r_act[:, GT * r:GT * r + GT, :]
                    act.activation(dst, summed[:, :, :], ACT.Silu).then_inc(s["silu"], 1)

                def log1p(self, n):
                    if n == 0:
                        act.wait_ge(s["half_free"], Y_READ)
                        act.activation(k_end[:, :, :], cum[:, :, :], ACT.Abs).then_inc(log1p_steps, 1)
                    if n == 1:
                        act.wait_ge(log1p_steps, 1)
                        act.activation(k_end[:, :, :], k_end[:, :, :], ACT.Exp, scale=-1.0)\
                           .then_inc(log1p_steps, 1)
                    if n == 2:
                        act.wait_ge(log1p_steps, 2)
                        act.activation(k_end[:, :, :], k_end[:, :, :], ACT.Ln, bias=1.0).then_inc(log1p_steps, 1)

                def exp_cum(self, n):
                    if n == 0:
                        act.wait_ge(cum_ready, 2)
                    act.activation(r_act[:, n * KEY // P:(n + 1) * KEY // P, :], cum[:, :, :], ACT.Exp,
                                   scale=(1.0 - 2.0 * n) / TAU).then_inc(exp_cum, 1)

                def tail_exp(self):
                    act.wait_ge(tail_ready, 1)
                    act.activation(k_end[:, :, :], k_end[:, :, :], ACT.Exp, scale=1.0 / TAU).then_inc(tail_exp, 1)

                def head_gain(self, h):
                    act.wait_ge(s["silu"], before("silu", R_GROUPS[h]) + 1)
                    for e in range(GT):
                        tile = r_act[:, GT * h + e, :]
                        ins = act.activation(tile, tile, ACT.Copy, scale=vec[:, V_HEAD + e:V_HEAD + e + 1])
                    ins.then_inc(head_gained, 1)

                def head_copy(self, h):
                    act.wait_ge(head_done, h + 1)
                    act.wait_ge(s["half_free"], HEAD_GROUPS[h])
                    act.activation(head_out[h], packed(HEAD_GROUPS[h] % 2, GT), ACT.Copy)\
                       .then_inc(s["half_free"], 1)

                def head_square(self, h):
                    act.wait_ge(s["half_free"], HEAD_GROUPS[h] + 1)
                    if h == 3:
                        act.wait_ge(head_sumsq, 2)
                    act.activation(head_sq[h], head_out[h], ACT.Square).then_inc(head_squares, 1)

                def head_root(self, pair, at):
                    act.wait_ge(head_ms, pair + 1)
                    act.activation(head_norm(pair), head_norm(pair), ACT.Sqrt).then_inc(head_root, 1)

                def gain_y(self, tiles):
                    for t in tiles:
                        ins = act.activation(y_gain[:, t, :], xT[:, t, :], ACT.Copy,
                                             scale=vec[:, V_FINAL + t:V_FINAL + t + 1])
                    ins.then_inc(y_gained, 1)

                def copy_y(self, j):
                    act.wait_ge(turned, 4 + j + 1)
                    act.activation(y_tok[:, 0, j * GW:(j + 1) * GW], y_turned(j, 0), ACT.Copy)\
                       .then_inc(y_copied[0], 1)

                def last_group(self):
                    act.wait_ge(s["sumsq"], before("sumsq", LAST))
                    act.activation(sum_group[:, 0:1], mean_x[:, 0:1], ACT.Sqrt)
                    for a in range(2):
                        act.wait_ge(last_added, a + 1)
                        act.activation(work[:, 2 * a:2 * a + 2, :], xT[:, DT - GT + 2 * a:DT - GT + 2 * a + 2, :],
                                       ACT.Square).then_inc(last_squares, 1)
                        self.gain_y(range(DT - GT + 2 * a, DT - GT + 2 * a + 2))

                def last_norm(self):
                    act.wait_ge(ms_ready, 5)
                    act.activation(rstd[:, T:T + 2], rstd[:, T:T + 2], ACT.Sqrt).then_inc(root_ready, 1)

                def scale_y(self):
                    act.wait_ge(rstd_ready, 5)
                    act.wait_ge(y_copied[0], 3)
                    for j in range(4):
                        cols = y_tok[:, 0, j * GW:(j + 1) * GW]
                        if j == 3:
                            act.wait_ge(turned, 4 + 4)
                        act.activation(cols, y_turned(3, 0) if j == 3 else cols, ACT.Copy,
                                       scale=rstd[:, T:T + 1]).then_inc(y_scaled[0], 1)

            whole_program(act, split, Scalar())

        @block.vector
        def _(dve):
            wide_rstd = rstd[:, 0:T].unsqueeze(1).to_broadcast([P, GT, T])
            wide_rstd_sq = rstd_sq[:, :].unsqueeze(1).to_broadcast([P, GT, T])

            def split(g, a, b, turn, stride):
                for n in range(a, b):
                    i, more = sub_number(g, n, turn, stride)
                    dve.wait_ge(hi_ready, i + 1 + more)
                    dve.tensor_tensor(w_lo[:, i % SLOTS], raw_view(i), w_hi[:, i % SLOTS].bitcast(f32),
                                      ALU.subtract).then_inc(lo_ready, 1)

            def add_parts(at, out=None, half=None):
                dve.wait_ge(sub_done, at.subs_done())
                dve.tensor_reduce(summed[:, :, :], two_parts(at.half), AX.X, ALU.add).then_inc(s["half_free"], 1)
                dve.wait_ge(s["half_free"], at.groups_done(1))

            class Vector(Steps):
                def ingest_x(self, at, j):
                    dve.wait_ge(turned, j + 1)
                    dve.tensor_copy(xT[:, GT * j:GT * j + GT, :], x_turned(j)).then_inc(s["half_free"], 1)
                    if j == 0:
                        dve.wait_ge(vectors_turned, 1)
                        dve.tensor_copy(vec[:, 0:P], bank(1, 3)[:, 0:P]).then_inc(vectors_ready, 1)

                def add_x(self, at, tile0):
                    if at.g == first_of("gla_out"):
                        dve.wait_ge(s["silu"], at.value("silu", 0))
                    add_parts(at)
                    dve.tensor_tensor(xT[:, tile0:tile0 + GT, :], xT[:, tile0:tile0 + GT, :], summed[:, :, :],
                                      ALU.add).then_inc(s["x_added"], 1)

                def split_x(self, at, tile0, norm):
                    if norm < 4:
                        if GROUPS[at.g][0] == "ingest":
                            dve.wait_ge(vectors_ready, 1)
                            dve.wait_ge(s["half_free"], at.groups_done(1))
                        dve.wait_ge(s["xs_hi"], at.value("xs_hi", 1))
                        for t in range(tile0, tile0 + GT):
                            ins = dve.scalar_tensor_tensor(
                                out=xs[:, t, T:2 * T], in0=xT[:, t, :],
                                scalar=vec[:, GAIN[norm] + t:GAIN[norm] + t + 1],
                                in1=xs[:, t, 0:T].bitcast(f32), op0=ALU.mult, op1=ALU.subtract)
                        ins.then_inc(s["xs_ready"], 1)

                def square_x(self, at, tile0, norm):
                    dve.wait_ge(s["squares"], at.value("squares", 1))
                    out, done = (sum_group, group_summed) if tile0 else (sum_x, s["sumsq"])
                    dve.tensor_reduce(out[:, :], work[:, :, :].rearrange("p a t -> p t a"), AX.X, ALU.add)\
                       .then_inc(done, 1)
                    if tile0:
                        dve.wait_ge(group_summed, 3 * norm + tile0 // GT)
                        dve.wait_ge(s["sumsq"], at.value("sumsq", 0))
                        dve.tensor_tensor(sum_x[:, :], sum_x[:, :], sum_group[:, :], ALU.add)\
                           .then_inc(s["sumsq"], 1)

                def more_vectors(self):
                    dve.wait_ge(vectors_turned, 2)
                    dve.tensor_copy(vec[:, P:], bank(1, 3)[:, P:V_HEAD + DV // P]).then_inc(vectors_ready, 1)

                def norm(self, n):
                    half = (first_of(("conv_in", "ffn0_in0", "gla_in", "ffn1_in0")[n]) + (n > 0)) % 2
                    if n == 2:
                        dve.memset(w_gate2[:, :], 0.0).then_inc(gate2_padded, 1)
                    dve.wait_ge(mean_done, n + 1)
                    dve.tensor_scalar(rstd[:, :], bank(half, 0)[:, 0:T + 2], EPS, None, ALU.add)\
                       .then_inc(ms_ready, 1)
                    dve.wait_ge(root_ready, n + 1)
                    dve.reciprocal(rstd[:, :], rstd[:, :]).then_inc(rstd_ready, 1)
                    dve.wait_ge(rstd_ready, n + 1)
                    if n == 0:
                        dve.tensor_tensor(rstd_sq[:, :], rstd[:, 0:T], rstd[:, 0:T], ALU.mult)\
                           .then_inc(rstd_sq_ready, 1)
                        dve.memset(conv_in[:, :, 0:2], 0.0).then_inc(conv_edge, 1)
                        dve.wait_ge(rstd_sq_ready, 1)
                        dve.wait_ge(conv_edge, 1)

                def add_conv_c(self, at):
                    add_parts(at)

                def scale_conv_c(self, at):
                    dve.tensor_tensor(conv_gate[:, :, :], summed[:, :, :], wide_rstd_sq, ALU.mult)\
                       .then_inc(s["scaled"], 1)

                def conv_u(self, at):
                    add_parts(at)
                    dve.wait_ge(s["scaled"], at.value("scaled", 0))
                    dve.tensor_tensor(conv_in[:, :, 2:], summed[:, :, :], conv_gate[:, :, :], ALU.mult)\
                       .then_inc(s["scaled"], 1)

                def conv_tap(self, at, tap):
                    j = (at.g - first_of("conv_in")) // 3
                    if tap == 0:
                        dve.wait_ge(s["scaled"], at.value("scaled", 1))
                    else:
                        dve.wait_ge(s["taps"], at.value("taps", tap))
                    for t in range(GT):
                        col = V_CONV + tap * DT + GT * j + t
                        w = vec[:, col:col + 1]
                        if tap == 0:
                            ins = dve.tensor_scalar(conv_y[:, t, :], conv_in[:, t, 0:T], w, None, ALU.mult)
                        else:
                            ins = dve.scalar_tensor_tensor(out=conv_y[:, t, :], in0=conv_in[:, t, tap:tap + T],
                                                           scalar=w, in1=conv_y[:, t, :], op0=ALU.mult, op1=ALU.add)
                    ins.then_inc(s["taps"], 1)

                def split_mid(self, at, tiles):
                    dve.wait_ge(s["mid_hi"], at.value("mid_hi", 1))
                    dve.tensor_tensor(mid[:, tiles, T:2 * T], work[:, :, :], mid[:, tiles, 0:T].bitcast(f32),
                                      ALU.subtract).then_inc(s["mid_ready"], 1)

                def conv_b(self, at):
                    add_parts(at)
                    dve.tensor_tensor(summed[:, :, :], summed[:, :, :], wide_rstd, ALU.mult)\
                       .then_inc(s["scaled"], 1)
                    dve.wait_ge(s["scaled"], at.value("scaled", 1))
                    dve.wait_ge(s["taps"], at.value("taps", 0))
                    dve.tensor_tensor(work[:, :, :], summed[:, :, :], conv_y[:, :, :], ALU.mult)\
                       .then_inc(s["product"], 1)

                def normed(self, at, r=None):
                    if r:
                        dve.wait_ge(s["silu"], at.value("silu", 0))
                    add_parts(at)
                    dve.tensor_tensor(summed[:, :, :], summed[:, :, :], wide_rstd, ALU.mult)\
                       .then_inc(s["scaled"], 1)

                def up(self, at):
                    dve.wait_ge(s["silu"], at.value("silu", 0))
                    add_parts(at)
                    dve.tensor_tensor(summed[:, :, :], summed[:, :, :], wide_rstd, ALU.mult)\
                       .then_inc(s["scaled"], 1)
                    dve.wait_ge(s["scaled"], at.value("scaled", 1))
                    dve.tensor_tensor(work[:, :, :], work[:, :, :], summed[:, :, :], ALU.mult)\
                       .then_inc(s["product"], 1)

                def key(self, at, j):
                    add_parts(at)
                    dve.tensor_tensor(k_t[:, GT * j:GT * j + GT, :], summed[:, :, :], wide_rstd, ALU.mult)\
                       .then_inc(s["scaled"], 1)

                def query(self, at, j):
                    add_parts(at)
                    dve.scalar_tensor_tensor(out=q_t[:, GT * j:GT * j + GT, :], in0=summed[:, :, :],
                                             scalar=DK ** -0.5, in1=wide_rstd, op0=ALU.mult, op1=ALU.mult)\
                       .then_inc(s["scaled"], 1)

                def zed(self, at):
                    dve.memset(reset[:, :], 1.0).then_inc(reset_ready, 1)
                    dve.wait_ge(reset_ready, 1)
                    dve.memset(reset[:, 0:T:CHUNK], 0.0).then_inc(reset_ready, 1)
                    dve.wait_ge(sub_done, at.subs_done())
                    dve.tensor_reduce(summed[:, 0, :], bank(at.half, 0).rearrange("p (h t) -> p t h", h=2),
                                      AX.X, ALU.add).then_inc(s["half_free"], 1)
                    dve.wait_ge(s["half_free"], at.groups_done(1))
                    dve.tensor_tensor(zT[:, :], summed[:, 0, :], rstd[:, 0:T], ALU.mult)\
                       .then_inc(s["scaled"], 1)

                def logits(self, at):
                    dve.wait_ge(logits_done, 1)
                    for t in range(KEY // P):
                        ins = dve.tensor_scalar(cum[:, t, :], packed(at.half, 8)[:, t, :],
                                                vec[:, V_BIAS + t:V_BIAS + t + 1], None, ALU.add)
                    ins.then_inc(s["half_free"], 1)

                def log_decay(self):
                    dve.wait_ge(log1p_steps, 3)
                    dve.scalar_tensor_tensor(out=k_end[:, :, :], in0=cum[:, :, :], scalar=0.0, in1=k_end[:, :, :],
                                             op0=ALU.min, op1=ALU.subtract).then_inc(log_decay_ready, 1)

                def running_sum(self, tiles):
                    dve.wait_ge(log_decay_ready, 1)
                    dve.wait_ge(reset_ready, 2)
                    for t in tiles:
                        ins = dve.tensor_tensor_scan(cum[:, t, :], reset[:, :], k_end[:, t, :], 0.0,
                                                     ALU.mult, ALU.add)
                    ins.then_inc(cum_ready, 1)

                def tail(self):
                    chunks = cum[:, :, :].rearrange("p a (n c) -> p (a n) c", c=CHUNK)
                    dve.wait_ge(cum_ready, 2)
                    dve.tensor_tensor(k_end[:, :, :].rearrange("p a (n c) -> p (a n) c", c=CHUNK),
                                      chunks[:, :, CHUNK - 1:CHUNK].to_broadcast([P, KEY // P * NCHUNK, CHUNK]),
                                      chunks, ALU.subtract).then_inc(tail_ready, 1)
                    dve.wait_ge(exp_cum, 1)
                    dve.tensor_copy(decay[:, :, :], r_act[:, 0:KEY // P, CHUNK - 1::CHUNK]).then_inc(decay_ready, 1)

                def keys_end(self):
                    dve.wait_ge(tail_exp, 1)
                    dve.tensor_tensor(k_end[:, :, :], k_end[:, :, :], k_t[:, :, :], ALU.mult).then_inc(keys_ready, 1)

                def keys_near(self):
                    dve.wait_ge(exp_cum, 2)
                    dve.tensor_tensor(k_t[:, :, :], k_t[:, :, :], r_act[:, KEY // P:, :], ALU.mult)\
                       .then_inc(keys_ready, 1)

                def queries_near(self):
                    dve.tensor_tensor(q_t[:, :, :], q_t[:, :, :], r_act[:, 0:KEY // P, :], ALU.mult)\
                       .then_inc(q_ready, 1)

                def queries_far(self):
                    def over(n):
                        return decay[:, :, n:n + 1].to_broadcast([P, KEY // P, CHUNK])

                    dve.wait_ge(q_ready, 1)
                    dve.wait_ge(decay_ready, 1)
                    dve.tensor_tensor(q_far[:, :, 0, :], q_t[:, :, 2 * CHUNK:3 * CHUNK], over(1), ALU.mult)\
                       .then_inc(q_far_steps, 1)
                    dve.tensor_tensor(q_far[:, :, 2, :], q_t[:, :, 3 * CHUNK:], over(2), ALU.mult)\
                       .then_inc(q_far_steps, 1)
                    dve.wait_ge(q_far_steps, 2)
                    dve.tensor_tensor(q_far[:, :, 1, :], q_far[:, :, 2, :], over(1), ALU.mult)\
                       .then_inc(q_far_steps, 1)

                def value(self, at, j):
                    dve.wait_ge(sub_done, at.subs_done())
                    for m in range(2):
                        ins = dve.tensor_scalar(v_tok[:, m, j * GW:(j + 1) * GW], bank(at.half, m),
                                                rstd[:, T + m:T + m + 1], None, ALU.mult)
                    ins.then_inc(s["half_free"], 1)

                def scores(self, at):
                    dve.wait_ge(scores_done, 1)
                    banks = ps[:, 4 * at.half:4 * at.half + 4, :]
                    for rows, cols in ((slice(0, CHUNK), slice(0, T)), (slice(CHUNK, P), slice(CHUNK, T)),
                                       (slice(0, CHUNK), slice(T, 3 * P)),
                                       (slice(CHUNK, P), slice(T + CHUNK, 3 * P))):
                        ins = dve.tensor_copy(att[rows, :, cols], banks[rows, :, cols])
                    ins.then_inc(s["half_free"], 1)

                def head_sumsq(self, h):
                    dve.wait_ge(head_squares, h + 1)
                    dve.tensor_reduce(q_t[:, h, :], head_sq[h].rearrange("p a t -> p t a"), AX.X, ALU.add)\
                       .then_inc(head_sumsq, 1)

                def head_root(self, pair, at):
                    dve.wait_ge(head_mean, 2 * pair + 2)
                    dve.tensor_scalar(head_norm(pair), ps[:, 4 * at.half + 2:4 * at.half + 4, 0:T], EPS, None,
                                      ALU.add).then_inc(head_ms, 1)

                def head_rstd(self, h):
                    dve.wait_ge(head_root, h // 2 + 1)
                    dve.reciprocal(q_t[:, HEADS + h, :], q_t[:, HEADS + h, :]).then_inc(head_rstd, 1)

                def head_gated(self, h):
                    dve.wait_ge(head_squares, h + 1)
                    dve.wait_ge(head_gained, h + 1)
                    dve.tensor_tensor(head_out[h], head_out[h], r_act[:, GT * h:GT * h + GT, :], ALU.mult)\
                       .then_inc(head_gated, 1)

                def head_scaled(self, h):
                    dve.wait_ge(head_rstd, h + 1)
                    dve.wait_ge(head_gated, h + 1)
                    if h == 0:
                        dve.wait_ge(head_sumsq, 1)
                    else:
                        dve.wait_ge(s["mid_ready"], before("mid_ready", HEAD_GROUPS[h]))
                    wide = q_t[:, HEADS + h, :].unsqueeze(1).to_broadcast([P, GT, T])
                    dve.tensor_tensor(work[:, :, :], head_out[h], wide, ALU.mult).then_inc(s["product"], 1)

                def copy_y(self, j):
                    dve.wait_ge(turned, 4 + j + 1)
                    dve.tensor_copy(y_tok[:, 1, j * GW:(j + 1) * GW], y_turned(j, 1)).then_inc(y_copied[1], 1)

                def last_group(self):
                    dve.wait_ge(sub_done, sub_before(LAST + 1))
                    for a in range(2):
                        part = slice(2 * a, 2 * a + 2)
                        tiles = slice(DT - GT + 2 * a, DT - GT + 2 * a + 2)
                        parts = two_parts(LAST % 2)[:, part]
                        dve.tensor_tensor(xT[:, tiles, :], xT[:, tiles, :], parts[:, :, :, 0], ALU.add)\
                           .then_inc(last_hi_added, 1)
                        dve.wait_ge(last_hi_added, a + 1)
                        dve.tensor_tensor(xT[:, tiles, :], xT[:, tiles, :], parts[:, :, :, 1], ALU.add)\
                           .then_inc(last_added, 1)

                def last_norm(self):
                    dve.wait_ge(mean_done, 5)
                    dve.tensor_scalar(rstd[:, T:T + 2].unsqueeze(2), y_means[:, :, 0:1], EPS, None, ALU.add)\
                       .then_inc(ms_ready, 1)
                    dve.wait_ge(root_ready, 5)
                    dve.reciprocal(rstd[:, T:T + 2], rstd[:, T:T + 2]).then_inc(rstd_ready, 1)

                def scale_y(self):
                    dve.wait_ge(rstd_ready, 5)
                    dve.wait_ge(y_copied[1], 3)
                    for j in range(4):
                        cols = y_tok[:, 1, j * GW:(j + 1) * GW]
                        if j == 3:
                            dve.wait_ge(turned, 4 + 4)
                        dve.tensor_scalar(cols, y_turned(3, 1) if j == 3 else cols, rstd[:, T + 1:T + 2], None,
                                          ALU.mult).then_inc(y_scaled[1], 1)

            whole_program(dve, split, Vector())

        @block.tensor
        def _(pe):
            def half_is_free(g, more=0):
                if g > first_of("conv_in"):
                    pe.wait_ge(s["half_free"], g - 1 + more)

            def project(g, operand, ready=None, turn=0, stride=0, before_sub=None, by_token=False):
                subs = GROUPS[g][1]
                half_is_free(g, turn * stride if stride else 0)
                for n in range(subs):
                    if before_sub and n in before_sub:
                        before_sub[n]()
                    i, more = sub_number(g, n, turn, stride)
                    if ready and n % 2 == 0:
                        pe.wait_ge(ready[0], ready[1] + n // 2 + 1)
                    pe.wait_ge(lo_ready, i + 1 + more)
                    for kk in range(SUB_K):
                        k = n * SUB_K + kk
                        start, stop = k == 0, k == subs * SUB_K - 1
                        hi, lo = w_hi[:, i % SLOTS, kk, :], w_lo[:, i % SLOTS, kk, :]
                        if by_token:
                            for m in range(2):
                                x_hi = operand[:, k, m * P:(m + 1) * P]
                                x_lo = operand[:, k, T + m * P:T + (m + 1) * P]
                                pe.matmul(bank(g % 2, m), x_hi, lo, start=start, stop=False)
                                pe.matmul(bank(g % 2, m), x_lo, hi, start=False, stop=False)
                                mm = pe.matmul(bank(g % 2, m), x_hi, hi, start=False, stop=stop)
                        else:
                            for o in range(GT):
                                cols = slice(o * P, (o + 1) * P)
                                pe.matmul(bank(g % 2, o), hi[:, cols], operand[:, k, :], start=start, stop=False)
                                mm = pe.matmul(bank(g % 2, o)[:, T:2 * T], lo[:, cols], operand[:, k, 0:T],
                                               start=False, stop=stop)
                    mm.then_inc(sub_done, 1)

            def mean_square(n, half):
                pe.wait_ge(s["sumsq"], 4 * (n + 1))
                pe.matmul(bank(half, 0)[:, 0:T], mean_x[:, :], sum_x[:, :], start=True, stop=True)
                for m in range(2):
                    mm = pe.matmul(bank(half, 0)[:, T + m:T + m + 1], sum_x[:, m * P:(m + 1) * P], mean_x[:, 0:1],
                                   start=True, stop=True)
                mm.then_inc(mean_done, 1)

            def first_group(g, norm):
                project(g, xs, ready=(s["xs_ready"], 4 * norm),
                        before_sub={MEAN_SUB: lambda: mean_square(norm, (g + 1) % 2)})
                pe.wait_ge(ms_ready, norm + 1)

            def turn_x(j):
                if j >= 2:
                    pe.wait_ge(s["half_free"], j - 1)
                pe.wait_ge(x_loaded[j], 16)
                for t in range(GT):
                    for m in range(2):
                        mm = pe.transpose(x_turned(j)[:, t, m * P:(m + 1) * P],
                                          x_tok[:, m, (GT * j + t) * P:(GT * j + t + 1) * P], ident[:, :])
                mm.then_inc(turned, 1)

            def turn_rows_b():
                rows = KEY // P + DV // P
                pe.wait_ge(rows_b_loaded, 2 * 16)
                pe.wait_ge(s["half_free"], 4)
                pe.transpose(bank(1, 3)[:, P:P + rows], rows_b[:, :], ident[0:rows, 0:rows])\
                  .then_inc(vectors_turned, 1)

            pe.wait_ge(consts_ready, 4)
            turn_x(0)
            pe.wait_ge(rows_a_loaded, 4 * 16)
            pe.transpose(bank(1, 3)[:, 0:P], rows_a[:, :], ident[:, :]).then_inc(vectors_turned, 1)
            pe.wait_ge(vectors_ready, 1)
            turn_x(1)

            g = first_of("conv_in")
            project(g, xs, ready=(s["xs_ready"], 0),
                    before_sub={1: lambda: turn_x(2), 3: lambda: turn_x(3), 6: turn_rows_b})
            pe.wait_ge(vectors_ready, 2)
            project(g + 1, xs, before_sub={3: lambda: (pe.wait_ge(s["half_free"], g + 1), mean_square(0, g % 2))})
            pe.wait_ge(ms_ready, 1)
            with pe.Fori(0, (count_of("conv_in") - 2) // 2) as i:
                for q in range(2):
                    project(g + 2 + q, xs, turn=i, stride=2)
            g = first_of("conv_out")
            with pe.Fori(0, 2) as i:
                for q in range(2):
                    project(g + q, mid, ready=(s["mid_ready"], before("mid_ready", g) - 4), turn=i, stride=2)

            def turn_y_tiles(j, tiles):
                for t in tiles:
                    for m in range(2):
                        mm = pe.transpose(y_turned(j, m)[:, t * P:(t + 1) * P],
                                          y_gain[:, GT * j + t, m * P:(m + 1) * P], ident[:, :])
                return mm

            def turn_y(j):
                if j == 0:
                    pe.wait_ge(s["half_free"], LAST)
                if j == 2:
                    pe.wait_ge(y_copied[0], 1)
                    pe.wait_ge(y_copied[1], 1)
                pe.wait_ge(y_gained, j + 1)
                turn_y_tiles(j, range(GT)).then_inc(turned, 1)

            def ffn(layer):
                for n, pairs in enumerate(PIECES):
                    g = first_of(f"ffn{layer}_in{n}")
                    done = 0
                    if n == 0:
                        first_group(g, 2 * layer + 1)
                        project(g + 1, xs)
                        done = 2
                    with pe.Fori(0, pairs - done // 2) as i:
                        for q in range(2):
                            project(g + done + q, xs, turn=i, stride=2)
                    g = first_of(f"ffn{layer}_out{n}")
                    ready = (s["mid_ready"], before("mid_ready", g) - pairs)
                    if g + 3 < LAST:
                        with pe.Fori(0, 2) as i:
                            for q in range(2):
                                project(g + q, mid, ready=ready, turn=i, stride=2)
                    else:
                        for q in range(3):
                            project(g + q, mid, ready=ready)
                        project(LAST, mid, ready=ready, before_sub={2: lambda: (turn_y(0), turn_y(1)),
                                                                    5: lambda: turn_y(2)})

            ffn(0)

            g = first_of("gla_in")
            K0, Z, K1, Y, Q0, Q1, V0, V1, V2, V3, R0, S, R1, H0, H1, R2, H2, H3, R3 = \
                range(first_of("gla_in"), first_of("gla_out"))
            first_group(K0, 2)
            half_is_free(Z)
            for n in range(2):
                i = sub_before(Z) + n
                pe.wait_ge(lo_ready, i + 1)
                hi = w_hi[:, i % SLOTS].rearrange("p a n -> p (a n)").rearrange("p (k n) -> p k n", n=P)
                lo = w_lo[:, i % SLOTS].rearrange("p a n -> p (a n)").rearrange("p (k n) -> p k n", n=P)
                for kk in range(DT // 2):
                    k = n * DT // 2 + kk
                    pe.matmul(bank(Z % 2, 0), hi[:, kk, :], xs[:, k, :], start=k == 0, stop=False)
                    mm = pe.matmul(bank(Z % 2, 0)[:, T:2 * T], lo[:, kk, :], xs[:, k, 0:T], start=False,
                                   stop=k == DT - 1)
                mm.then_inc(sub_done, 1)
            project(K1, xs)
            half_is_free(Y)
            pe.wait_ge(s["scaled"], before("scaled", Z) + 1)
            pe.wait_ge(gate2_loaded, 16)
            for t in range(KEY // P):
                mm = pe.matmul(packed(Y % 2, 8)[:, t, :], w_gate2[:, t * P:(t + 1) * P], zT[:, :],
                               start=True, stop=True)
            mm.then_inc(logits_done, 1)
            project(Q0, xs)
            project(Q1, xs)
            for j in range(4):
                project(V0 + j, xs, by_token=True)
            project(R0, xs)

            half_is_free(S)
            pe.wait_ge(keys_ready, 2)
            pe.wait_ge(q_far_steps, 3)
            for h in range(HEADS):
                for m in range(NCHUNK):
                    keys = slice(m * CHUNK, (m + 1) * CHUNK)
                    rows = slice(CHUNK * (m % 2), CHUNK * (m % 2) + CHUNK)
                    base = T - P if m >= 2 else 0
                    jobs = [(k_t, m, lambda d, m=m: q_t[:, d, m * CHUNK:(m + 1) * CHUNK], 1)]
                    if m + 1 < NCHUNK:
                        jobs.append((k_end, m + 1, lambda d, m=m: q_t[:, d, (m + 1) * CHUNK:(m + 2) * CHUNK], 1))
                    if m == 0:
                        jobs.append((k_end, 2, lambda d: q_far[:, d, 0:2, :].rearrange("p a c -> p (a c)"), 2))
                    if m == 1:
                        jobs.append((k_end, 3, lambda d: q_far[:, d, 2, :], 1))
                    for src, c, query, width in jobs:
                        dst = bank(S % 2, h)[rows, base + c * CHUNK:base + (c + width) * CHUNK]
                        for half in range(2):
                            d = 2 * h + half
                            mm = pe.matmul(dst, src[:, d, keys], query(d), start=half == 0, stop=half == 1)
            mm.then_inc(scores_done, 1)

            def head(g, h):
                half_is_free(g)
                if h == 0:
                    pe.wait_ge(att_masked, 2)
                for e in range(GT):
                    cols = slice(h * DV + e * P, h * DV + (e + 1) * P)
                    dst = packed(g % 2, GT)[:, e, :]
                    pe.matmul(dst, v_tok[:, 0, cols], att[:, h, 0:T], start=True, stop=False)
                    mm = pe.matmul(dst[:, P:T], v_tok[:, 1, cols], att[:, h, T:3 * P], start=False, stop=True)
                mm.then_inc(head_done, 1)

            def head_mean_squares(g, pair):
                pe.wait_ge(head_sumsq, 2 * pair + 2)
                for h in (2 * pair, 2 * pair + 1):
                    pe.matmul(bank(g % 2, 2 + h % 2)[:, 0:T], mean_head[:, :], q_t[:, h, :], start=True, stop=True)\
                      .then_inc(head_mean, 1)

            project(R1, xs)
            head(H0, 0)
            head(H1, 1)
            project(R2, xs, before_sub={HEAD_MEAN_SUB: lambda: head_mean_squares(H1, 0)})
            head(H2, 2)
            head(H3, 3)
            pe.wait_ge(head_ms, 1)
            project(R3, xs, before_sub={HEAD_MEAN_SUB: lambda: head_mean_squares(H3, 1)})
            pe.wait_ge(head_ms, 2)
            g = first_of("gla_out")
            with pe.Fori(0, 2) as i:
                for q in range(2):
                    project(g + q, mid, ready=(s["mid_ready"], before("mid_ready", g) - 4), turn=i, stride=2)
            ffn(1)

            for m in range(2):
                pe.wait_ge(y_copied[m], 3)
            pe.wait_ge(s["sumsq"], before("sumsq", LAST))
            for m in range(2):
                pe.matmul(y_means[:, m, 0:1], sum_x[:, m * P:(m + 1) * P], mean_x[:, 0:1], start=True, stop=False)
            for a in range(2):
                pe.wait_ge(last_squares, a + 1)
                for t in (2 * a, 2 * a + 1):
                    for m in range(2):
                        mm = pe.matmul(y_means[:, m, 0:1], work[:, t, m * P:(m + 1) * P], mean_x[:, 0:1],
                                       start=False, stop=t == GT - 1)
            mm.then_inc(mean_done, 1)
            pe.wait_ge(y_gained, 3 + 2)
            turn_y_tiles(3, range(GT)).then_inc(turned, 1)


def kernel(**inputs):
    import numpy as np
    import concourse.bacc as bacc
    from concourse.bass_utils import run_bass_kernel_spmd

    shapes = {
        "x": (T, D), "norm_mix": (2, D), "norm_ffn": (2, D), "norm_final": (D,), "conv_w_in": (D, 3 * D),
        "conv_w": (3, D), "conv_w_out": (D, D), "gla_w_in": (D, GLA_COLS), "gla_w_gate2": (RANK, KEY),
        "gla_b_gate": (KEY,), "gla_norm": (DV,), "gla_w_out": (D, D), "ffn_w_in": (2, D, 2 * F),
        "ffn_w_out": (2, F, D),
    }
    nc = bacc.Bacc("TRN2", target_bir_lowering=False, num_devices=1)
    arrays, args = {}, []
    for name, shape in shapes.items():
        a = np.ascontiguousarray(inputs[name]).reshape(shape)
        arrays[f"in_{name}"] = a
        args.append(nc.dram_tensor(f"in_{name}", shape, mybir.dt.from_np(a.dtype), kind="ExternalInput").ap())
    args.append(nc.dram_tensor("trunk_out", (T, D), mybir.dt.float32, kind="ExternalOutput").ap())
    trunk(nc, *args)
    r = run_bass_kernel_spmd(nc, [arrays], core_ids=[0])
    return r.results[0]["trunk_out"].reshape(1, T, D)
```
